# Optimizing a Trainium2 kernel written in Bass

```python
import jax, jax.numpy as jnp
from jax import lax
import numpy as np

D_MODEL = 1024
BATCH = 1
SEQ = 1024
DEPTH = 2

CHUNK = 64
BRANCH_WIDTH = D_MODEL // 2
N_BRANCHES = 4
HEAD_DIM = 64
N_Q_HEADS = BRANCH_WIDTH // HEAD_DIM
N_KV_HEADS = 2
Q_PER_KV = N_Q_HEADS // N_KV_HEADS
KV_WIDTH = N_KV_HEADS * HEAD_DIM
WINDOW = 128
WINDOW_CHUNKS = WINDOW // CHUNK
ROPE_THETA = 10000.0
POOL_WINDOWS = (2, 4, 8, 16)
N_POOL_GROUPS = len(POOL_WINDOWS)
POOL_GROUP = BRANCH_WIDTH // N_POOL_GROUPS
SGU_CHUNK = 128
N_SGU_GROUPS = 4
SGU_GROUP = BRANCH_WIDTH // N_SGU_GROUPS
CONV_WIDTH = 31
EPS = 1e-6

_SIZES = (
    BRANCH_WIDTH, KV_WIDTH, KV_WIDTH, BRANCH_WIDTH,
    BRANCH_WIDTH, BRANCH_WIDTH,
    BRANCH_WIDTH, BRANCH_WIDTH, BRANCH_WIDTH,
    BRANCH_WIDTH, BRANCH_WIDTH, BRANCH_WIDTH,
    N_BRANCHES * D_MODEL,
)
IN_WIDTH = int(sum(_SIZES))
SPLIT_POINTS = tuple(int(v) for v in np.cumsum(_SIZES)[:-1])

kernel_name = "hybrid_parallel_gated_streaming_block"

def rms_norm(x, g):
    xf = x.astype(jnp.float32)
    y = xf * lax.rsqrt(jnp.mean(xf * xf, axis=-1, keepdims=True) + EPS)
    return (y * g.astype(jnp.float32)).astype(x.dtype)

def layer_norm(x, g, b):
    xf = x.astype(jnp.float32)
    mu = jnp.mean(xf, axis=-1, keepdims=True)
    xc = xf - mu
    y = xc * lax.rsqrt(jnp.mean(xc * xc, axis=-1, keepdims=True) + EPS)
    return (y * g.astype(jnp.float32) + b.astype(jnp.float32)).astype(x.dtype)

def rope_tables(seq):
    pos = jnp.arange(seq, dtype=jnp.float32)
    inv = 1.0 / (ROPE_THETA ** (jnp.arange(0, HEAD_DIM, 2, dtype=jnp.float32) / HEAD_DIM))
    ang = pos[:, None] * inv[None, :]
    return jnp.cos(ang), jnp.sin(ang)

def apply_rope(x, cos, sin):
    xf = x.astype(jnp.float32)
    x1, x2 = jnp.split(xf, 2, axis=-1)
    c = cos[None, :, None, :]
    s = sin[None, :, None, :]
    return jnp.concatenate([x1 * c - x2 * s, x2 * c + x1 * s], axis=-1).astype(x.dtype)

def window_attention(q, k, v, sinks):
    B, S = q.shape[0], q.shape[1]
    nc = S // CHUNK
    qb = q.reshape(B, nc, CHUNK, N_KV_HEADS, Q_PER_KV, HEAD_DIM)
    pad = ((0, 0), ((WINDOW_CHUNKS - 1) * CHUNK, 0), (0, 0), (0, 0))
    kp = jnp.pad(k, pad).reshape(B, nc + WINDOW_CHUNKS - 1, CHUNK, N_KV_HEADS, HEAD_DIM)
    vp = jnp.pad(v, pad).reshape(B, nc + WINDOW_CHUNKS - 1, CHUNK, N_KV_HEADS, HEAD_DIM)
    kb = jnp.concatenate([kp[:, i:i + nc] for i in range(WINDOW_CHUNKS)], axis=2)
    vb = jnp.concatenate([vp[:, i:i + nc] for i in range(WINDOW_CHUNKS)], axis=2)
    scale = HEAD_DIM ** -0.5
    s = jnp.einsum('bcqhgd,bckhd->bchgqk', qb, kb,
                   preferred_element_type=jnp.float32) * scale
    key_chunk = (jnp.arange(nc)[:, None] - (WINDOW_CHUNKS - 1)
                 + (jnp.arange(WINDOW) // CHUNK)[None, :])
    valid = key_chunk >= 0
    s = jnp.where(valid[None, :, None, None, None, :], s, -jnp.inf)
    sink = sinks.astype(jnp.float32).reshape(N_KV_HEADS, Q_PER_KV)[None, None, :, :, None, None]
    m = jnp.maximum(jnp.max(s, axis=-1, keepdims=True), sink)
    p = jnp.exp(s - m)
    p = p / (jnp.sum(p, axis=-1, keepdims=True) + jnp.exp(sink - m))
    o = jnp.einsum('bchgqk,bckhd->bcqhgd', p.astype(vb.dtype), vb)
    return o.reshape(B, S, N_Q_HEADS * HEAD_DIM)

def multiscale_pool(p, w_mix, scale):
    B, S, C = p.shape
    pf = p.astype(jnp.float32)
    cs = jnp.cumsum(pf, axis=1)
    t = jnp.arange(1, S + 1, dtype=jnp.float32)
    outs = []
    for gi, w in enumerate(POOL_WINDOWS):
        lo, hi = gi * POOL_GROUP, (gi + 1) * POOL_GROUP
        c = cs[..., lo:hi]
        lag = jnp.pad(c, ((0, 0), (w, 0), (0, 0)))[:, :S]
        mean = (c - lag) / jnp.minimum(t, float(w))[None, :, None]
        outs.append(mean - pf[..., lo:hi])
    pooled = jnp.stack(outs, axis=2).astype(p.dtype)
    mixed = jnp.einsum('bsgc,gcd->bsgd', pooled, w_mix).reshape(B, S, C)
    return mixed * scale

def spatial_gating(u, v, ln_g, ln_b, w_s, b_s):
    B, S, C = u.shape
    v = layer_norm(v, ln_g, ln_b)
    n = S // SGU_CHUNK
    vb = v.reshape(B, n, SGU_CHUNK, N_SGU_GROUPS, SGU_GROUP)
    blk = jnp.arange(SGU_CHUNK) // CHUNK
    mask = blk[None, :] <= blk[:, None]
    w = jnp.where(mask[None], w_s, jnp.zeros_like(w_s))
    mixed = jnp.einsum('gij,bnjgc->bnigc', w, vb) + b_s.T[None, None, :, :, None]
    return u * mixed.reshape(B, S, C)

def conformer_conv(a, b, conv_w, conv_b, ln_g, ln_b):
    h = a * jax.nn.sigmoid(b)
    C = h.shape[-1]
    h = lax.conv_general_dilated(h, conv_w[:, None, :].astype(h.dtype), window_strides=(1,),
                                 padding=[(CONV_WIDTH - 1, 0)],
                                 dimension_numbers=('NWC', 'WIO', 'NWC'),
                                 feature_group_count=C) + conv_b
    h = layer_norm(h, ln_g, ln_b)
    return jax.nn.silu(h)

def hybrid_layer(x, cos, sin, norm_g, w_in, q_norm_g, k_norm_g, attn_sinks, pool_mix, pool_scale,
                 sgu_ln_g, sgu_ln_b, sgu_w, sgu_b, conv_w, conv_b, conv_ln_g, conv_ln_b,
                 w_branch, w_out):
    B, S, D = x.shape
    h = rms_norm(x, norm_g)
    proj = h @ w_in
    (q, k, v, z_a, p_in, z_b, u, v_sgu, z_c, glu_a, glu_b, z_d,
     merge) = jnp.split(proj, SPLIT_POINTS, axis=-1)
    q = apply_rope(rms_norm(q.reshape(B, S, N_Q_HEADS, HEAD_DIM), q_norm_g), cos, sin)
    k = apply_rope(rms_norm(k.reshape(B, S, N_KV_HEADS, HEAD_DIM), k_norm_g), cos, sin)
    v = v.reshape(B, S, N_KV_HEADS, HEAD_DIM)
    o_a = window_attention(q, k, v, attn_sinks)
    o_b = multiscale_pool(p_in, pool_mix, pool_scale)
    o_c = spatial_gating(u, v_sgu, sgu_ln_g, sgu_ln_b, sgu_w, sgu_b)
    o_d = conformer_conv(glu_a, glu_b, conv_w, conv_b, conv_ln_g, conv_ln_b)
    branches = jnp.stack([o_a * jax.nn.silu(z_a), o_b * jax.nn.silu(z_b),
                          o_c * jax.nn.silu(z_c), o_d * jax.nn.silu(z_d)], axis=2)
    branch_out = jnp.einsum('bsnw,nwd->bsnd', branches, w_branch)
    gates = jax.nn.sigmoid(merge.reshape(B, S, N_BRANCHES, D))
    mixed = jnp.sum(gates * branch_out, axis=2)
    return x + mixed @ w_out

def setup_inputs(seed: int = 0) -> dict:
    key = jax.random.key(seed)
    ks = jax.random.split(key, 20)
    f32 = jnp.float32
    nrm = lambda k, shape, s: jax.random.normal(k, shape, f32) * s
    L, W = DEPTH, BRANCH_WIDTH
    return {
        "x": nrm(ks[0], (BATCH, SEQ, D_MODEL), 1.0),
        "norm_g": 1.0 + nrm(ks[1], (L, D_MODEL), 0.05),
        "w_in": nrm(ks[2], (L, D_MODEL, IN_WIDTH), D_MODEL ** -0.5),
        "q_norm_g": 1.0 + nrm(ks[3], (L, HEAD_DIM), 0.05),
        "k_norm_g": 1.0 + nrm(ks[4], (L, HEAD_DIM), 0.05),
        "attn_sinks": nrm(ks[5], (L, N_Q_HEADS), 0.5),
        "pool_mix": nrm(ks[6], (L, N_POOL_GROUPS, POOL_GROUP, POOL_GROUP), POOL_GROUP ** -0.5),
        "pool_scale": 1.0 + nrm(ks[7], (L, W), 0.1),
        "sgu_ln_g": 1.0 + nrm(ks[8], (L, W), 0.05),
        "sgu_ln_b": nrm(ks[9], (L, W), 0.02),
        "sgu_w": nrm(ks[10], (L, N_SGU_GROUPS, SGU_CHUNK, SGU_CHUNK), SGU_CHUNK ** -0.5),
        "sgu_b": 1.0 + nrm(ks[11], (L, N_SGU_GROUPS, SGU_CHUNK), 0.1),
        "conv_w": nrm(ks[12], (L, CONV_WIDTH, W), CONV_WIDTH ** -0.5),
        "conv_b": nrm(ks[13], (L, W), 0.02),
        "conv_ln_g": 1.0 + nrm(ks[14], (L, W), 0.05),
        "conv_ln_b": nrm(ks[15], (L, W), 0.02),
        "w_branch": nrm(ks[16], (L, N_BRANCHES, W, D_MODEL), W ** -0.5),
        "w_out": nrm(ks[17], (L, D_MODEL, D_MODEL), D_MODEL ** -0.5),
    }

def reference(x, norm_g, w_in, q_norm_g, k_norm_g, attn_sinks, pool_mix, pool_scale,
              sgu_ln_g, sgu_ln_b, sgu_w, sgu_b, conv_w, conv_b, conv_ln_g, conv_ln_b,
              w_branch, w_out):
    cos, sin = rope_tables(x.shape[1])
    h = x
    for l in range(DEPTH):
        h = hybrid_layer(h, cos, sin, norm_g[l], w_in[l], q_norm_g[l], k_norm_g[l], attn_sinks[l],
                         pool_mix[l], pool_scale[l], sgu_ln_g[l], sgu_ln_b[l], sgu_w[l], sgu_b[l],
                         conv_w[l], conv_b[l], conv_ln_g[l], conv_ln_b[l], w_branch[l], w_out[l])
    return h


_drawn_inputs = setup_inputs


def setup_inputs(seed=0):
    import zlib

    import numpy as np

    out = dict(_drawn_inputs(seed))
    spreads = {}
    factors = {'q_norm_g': 8.0,
     'k_norm_g': 8.0,
     'attn_sinks': 8.0,
     'sgu_ln_g': 3.358,
     'sgu_ln_b': 7.84,
     'conv_b': 5.627,
     'conv_ln_g': 3.896,
     'conv_ln_b': 8.0}
    for name, (base, spread) in spreads.items():
        noise = np.random.default_rng([zlib.crc32(name.encode()), seed]).standard_normal(out[name].shape)
        drawn = base * np.exp(spread * noise) if base else spread * noise
        out[name] = __import__('jax').numpy.asarray(drawn.astype(out[name].dtype))
    for name, factor in factors.items():
        out[name] = (out[name] * factor).astype(out[name].dtype)
    return out
```

```python
from contextlib import ExitStack

import concourse.bass as bass
from concourse import mybir
from concourse.alu_op_type import AluOpType as ALU

F32 = mybir.dt.float32
F32R = mybir.dt.float32r
ACT = mybir.ActivationFunctionType
AX = mybir.AxisListType
ds = bass.ds

P = 128
LAYERS = 2
D = 1024
SEQ = 1024
W = 512
HD = 64
CHUNK = 64
NCHUNK = SEQ // CHUNK
KT = D // P
WT = W // P
TT = SEQ // P
HALF = 512
NQT = 4
NPAIRS = TT * 2
TAPS = 31
PADC = TAPS + 1
POOL_W = (2, 4, 8, 16)
POOL_PAD = 16
EPS = 1e-6
SCALE = HD ** -0.5
NEG = -1e30

S_GLU, S_VS, S_U, S_QKV, S_ZC, S_MC, S_ZA, S_MA, S_P, S_ZB, S_MB, S_ZD, S_MD, S_OUT, STEPS = (
    0, 8, 12, 16, 22, 26, 42, 46, 62, 66, 70, 86, 90, 106, 114)
PAIR = STEPS // 2


def unit_bases():
    at, out = 0, {}
    for s in range(STEPS + 1):
        out[s] = at
        merge = any(a <= s < a + 16 for a in (S_MC, S_MA, S_MB, S_MD))
        at += 1 if merge and (s - S_MC) % 2 else 2
    return out


UB = unit_bases()
UNITS = UB[STEPS]
UK = 4
UW = UK * P
SLOTS = 4
RAWS = 2

C_G = 0
C_CW = C_G + KT
C_CB = C_CW + WT * TAPS
C_CLG = C_CB + WT
C_CLB = C_CLG + WT
C_PS = C_CLB + WT
C_SINK = C_PS + WT
C_N = C_SINK + 8
MAXS, NMAX, SDIFF, PSUM_, ESINK, DEN, RDEN = range(7)
R_G, R_B, R_BS, R_QK, R_N = 0, W, 2 * W, 3 * W, 3 * W + 2 * HD


def hybrid_block(nc, x, wstream, cols, rows, sgu_wt, pool_mix, rope, ident_in, mask_in, edge_in, out):
    ctx = ExitStack()
    with ctx:
        cursor = [(nc.sbuf_base + 63) // 64 * 64]

        def place(name, shape, dt, at=None):
            n = 4
            for v in shape[1:]:
                n *= v
            if at is None:
                at = cursor[0]
                cursor[0] = at + (n + 63) // 64 * 64
                assert cursor[0] <= nc.sbuf_usable_end, (name, cursor[0], nc.sbuf_usable_end)
            return nc.alloc_sbuf_tensor_at(name, shape, dt, offset=at)

        def sem(name):
            return ctx.enter_context(nc.semaphore(name))

        hhi = place("hhi", [P, KT, SEQ], F32R)
        hlo = place("hlo", [P, KT, SEQ], F32R)
        at_x = cursor[0]
        xm = place("xm", [P, KT, SEQ], F32)
        cosb = place("cosb", [P, TT, HD // 2], F32, at_x)
        sinb = place("sinb", [P, TT, HD // 2], F32, at_x + 1024)
        ropeb = place("ropeb", [P, 2, 4, TT, HD // 2], F32, at_x + 2048)
        tok = place("tok", [P, SEQ], F32, at_x + 10240)
        sqt = place("sqt", [P, SEQ], F32, at_x + 14336)
        rot = place("rot", [P, 2, SEQ], F32, at_x + 18432)
        rt1 = place("rt1", [P, W], F32, at_x + 26624)
        rt2 = place("rt2", [P, W], F32, at_x + 28672)
        at_b = cursor[0]
        bhi = place("bhi", [P, WT, SEQ], F32R)
        blo = place("blo", [P, WT, SEQ], F32R)
        rowb = place("rowb", [P, R_N], F32, at_b)
        sgt = place("sgt", [P, WT, P], F32, at_b + 7168)
        stmp = place("stmp", [P, SEQ], F32, at_b + 9216)
        rstd = place("rstd", [P, SEQ], F32, at_b + 13312)
        htmp = place("htmp", [P, 2, SEQ], F32, at_b + 17408)
        pmix = place("pmix", [P, WT, P], F32, at_b)
        edge = place("edge", [P, WT, POOL_PAD], F32, at_b + 2048)
        pool1 = place("pool1", [P, POOL_PAD + SEQ], F32, at_b + 2560)
        pool2 = place("pool2", [P, POOL_PAD + SEQ], F32, at_b + 2560 + 4160)
        pooled = place("pooled", [P, 2, SEQ], F32, at_b + 2560 + 8320)
        raw = place("raw", [P, RAWS, UW], F32)
        whi = place("whi", [P, SLOTS, UW], F32R)
        wlo = place("wlo", [P, SLOTS, UW], F32R)
        at_conv = cursor[0]
        conv = place("conv", [P, WT + 1, PADC + SEQ], F32)
        at_r2 = cursor[0]
        vs = place("vs", [P, TT, W], F32)
        qo = place("qo", [P, NQT, SEQ], F32, at_r2)
        csq = place("csq", [P, WT, SEQ], F32, at_r2)
        at_r3 = cursor[0]
        oc = place("oc", [P, WT, SEQ], F32)
        kt = place("kt", [P, SEQ], F32, at_conv)
        vt = place("vt", [P, TT, P], F32)
        xin = place("xin", [P, KT, SEQ], F32, at_r2)
        assert at_r3 == at_r2 + 16384
        ev = place("ev", [P, 2, POOL_PAD + SEQ], F32)
        EV = [ev[:, p, POOL_PAD:POOL_PAD + SEQ] for p in range(2)]
        qs = place("qs", [P, 2, NQT, CHUNK], F32, at_r3)
        ks = place("ks", [P, 2, P], F32, at_r3 + 2048)
        vst = place("vst", [P, 4, P], F32, at_r3 + 3072)
        prob = place("prob", [P, 8, P], F32, at_r3 + 5120)
        probt = place("probt", [P, 8, P], F32, at_r3 + 9216)
        st = place("st", [P, 8, 8], F32)
        stq = place("stq", [P, 2, NPAIRS], F32)
        stv = place("stv", [P, TT, 6], F32)
        mv = place("mv", [P, TT, 2], F32)
        allp = place("allp", [P, LAYERS, C_N], F32)
        par = place("par", [P, C_N], F32)
        nsink = place("nsink", [P, 8], F32)
        epst = place("epst", [P, 1], F32)
        ones = place("ones", [P, P], F32)
        ident = place("ident", [P, P], F32)
        mask = place("mask", [P, 2, CHUNK], F32)
        sumsq = place("sumsq", [P, SEQ], F32)

        acc = ctx.enter_context(nc.psum_tensor("acc", [P, 2, SEQ], F32))
        aux = ctx.enter_context(nc.psum_tensor("aux", [P, 2, SEQ], F32))

        const_loaded = sem("const_loaded")
        x_loaded = sem("x_loaded")
        x_copied = sem("x_copied")
        rows_loaded = sem("rows_loaded")
        mix_loaded = sem("mix_loaded")
        xin_loaded = sem("xin_loaded")
        x_stored = sem("x_stored")
        raw_loaded = [sem(f"raw_loaded{i}") for i in range(RAWS)]
        hi_split = sem("hi_split")
        unit_split = sem("unit_split")
        unit_used = sem("unit_used")
        acc_read = [sem(f"acc_read{p}") for p in range(2)]
        consts_made = sem("consts_made")
        par_ready = sem("par_ready")
        rms_summed = sem("rms_summed")
        rms_root = sem("rms_root")
        h_scaled = sem("h_scaled")
        h_hi = sem("h_hi")
        h_ready = sem("h_ready")
        turned = sem("turned")
        turn_read = sem("turn_read")
        sgu_var = sem("sgu_var")
        sgu_root = sem("sgu_root")
        vs_ready = sem("vs_ready")
        sgu_mixed = sem("sgu_mixed")
        sgu_read = sem("sgu_read")
        z_taken = sem("z_taken")
        gated = sem("gated")
        qk_meansq = sem("qk_meansq")
        qk_root = sem("qk_root")
        roped = sem("roped")
        rot_turned = sem("rot_turned")
        rot_read = sem("rot_read")
        staged = sem("staged")
        scored = sem("scored")
        rowmax = sem("rowmax")
        probs_ready = sem("probs_ready")
        normed = sem("normed")
        p_turned = sem("p_turned")
        pt_ready = sem("pt_ready")
        pv_done = sem("pv_done")
        o_ready = sem("o_ready")
        pooled_ready = sem("pooled_ready")
        pool_mixed = sem("pool_mixed")
        ob_ready = sem("ob_ready")
        conv_summed = sem("conv_summed")
        d_mean = sem("d_mean")
        d_centred = sem("d_centred")
        d_squared = sem("d_squared")
        d_sumsq = sem("d_sumsq")
        d_var = sem("d_var")
        d_root = sem("d_root")
        d_normed = sem("d_normed")
        d_act = sem("d_act")
        merged = sem("merged")
        mix_hi = sem("mix_hi")
        mix_ready = sem("mix_ready")
        xsq_ready = sem("xsq_ready")
        xsq_added = sem("xsq_added")
        rope_loaded = sem("rope_loaded")

        settled = sem("settled")

        block = ctx.enter_context(nc.Block())

        def used(L, s, k=0):
            return L * UNITS + (UB[s] + k)

        def settle(eng):
            eng.sem_inc(settled, 1)

        def wait_read(eng, L, s, more=0):
            eng.wait_ge(acc_read[s % 2], L * PAIR + more + (s // 2 + 2))

        @block.sync
        def _(sp):
            for t, src in ((allp, cols), (ident, ident_in), (mask, mask_in)):
                sp.dma_start(t[:], src).then_inc(const_loaded, 16)
            sp.dma_start(raw[:, 0, :], wstream[0]).then_inc(raw_loaded[0], 16)
            for k in range(KT):
                sp.dma_start(xm[:, k, :], x[k * P:(k + 1) * P, :]).then_inc(x_loaded, 16)
            sp.dma_start(raw[:, 1, :], wstream[1]).then_inc(raw_loaded[1], 16)
            with sp.Fori(1, LAYERS * UNITS // RAWS) as b:
                for i in range(RAWS):
                    sp.wait_ge(unit_split, b * RAWS + (i - RAWS + 1))
                    sp.dma_start(raw[:, i, :], wstream[b * RAWS + i]).then_inc(raw_loaded[i], 16)

        @block.gpsimd
        def _(pool):
            def split(i, loads, n, first):
                pool.wait_ge(raw_loaded[i % RAWS], loads * 16)
                if not first:
                    pool.wait_ge(unit_used, n - (SLOTS - 1))
                    settle(pool)
                nc.gpsimd.tensor_scalar(whi[:, i, :], raw[:, i % RAWS, :], 1.0, 0.0, ALU.mult,
                                        ALU.add).then_inc(hi_split, 1)
                pool.wait_ge(hi_split, n + 1)
                nc.gpsimd.tensor_tensor(wlo[:, i, :], raw[:, i % RAWS, :],
                                        whi[:, i, :].bitcast(F32), ALU.subtract).then_inc(unit_split, 1)

            for i in range(SLOTS):
                split(i, i // RAWS + 1, i, True)
            with pool.Fori(1, LAYERS * UNITS // SLOTS) as b:
                for i in range(SLOTS):
                    split(i, b * (SLOTS // RAWS) + (i // RAWS + 1), b * SLOTS + i, False)

        @block.tensor
        def _(pe):
            def unit(L, u, slot, kbase, p, src, first, last):
                hi, lo = src
                pe.wait_ge(unit_split, L * UNITS + u + 1)
                for k in range(UK):
                    wh = whi[:, slot, k * P:(k + 1) * P]
                    wl = wlo[:, slot, k * P:(k + 1) * P]
                    for n, (w, m) in enumerate(((wh, hi), (wh, lo), (wl, hi))):
                        for t in range(2):
                            mm = nc.tensor.matmul(
                                acc[:, p, t * HALF:(t + 1) * HALF], w,
                                m[:, kbase + k, t * HALF:(t + 1) * HALF],
                                start=first and k == 0 and n == 0,
                                stop=last and k == UK - 1 and n == 2)
                mm.then_inc(unit_used, 1)

            H = (hhi, hlo)
            B = (bhi, blo)

            def project(L, s, i=0, between=None, ready=None, su=0, sr=0):
                p = s % 2
                pe.wait_ge(acc_read[p], L * PAIR + sr + (s // 2 + 1))
                if ready:
                    pe.wait_ge(ready, L * KT + UK)
                unit(L, UB[s] + su, UB[s] % SLOTS, 0, p, H, True, False)
                if between:
                    between()
                if ready:
                    pe.wait_ge(ready, L * KT + KT)
                unit(L, UB[s] + 1 + su, (UB[s] + 1) % SLOTS, UK, p, H, False, True)

            def projects(L, s0, n, ready=None):
                with pe.Fori(0, n // 2) as it:
                    for i in range(2):
                        project(L, s0 + i, ready=ready, su=it * 4, sr=it)

            def merge(L, s0, nb, attention=None):
                with pe.Fori(0, 2) as it:
                    for i in range(4):
                        s = s0 + 2 * i
                        if attention:
                            attention(0, it, i)
                        project(L, s, su=it * 12, sr=it * 4)
                        if attention:
                            attention(1, it, i)
                        pe.wait_ge(gated, L * 16 + 4 * nb)
                        pe.wait_ge(acc_read[1], L * PAIR + it * 4 + (s // 2 + 1))
                        unit(L, UB[s + 1] + it * 12, UB[s + 1] % SLOTS, 0, 1, B, True, True)
                        if attention:
                            attention(2, it, i)

            def turn(L, n, prev):
                p = n % 2
                prev()
                for t in range(TT):
                    mm = nc.tensor.transpose(aux[:, p, t * P:(t + 1) * P],
                                             EV[p][:, t * P:(t + 1) * P], ident[:])
                mm.then_inc(turned, 1)

            def turn_v(L, j):
                def prev():
                    wait_read(pe, L, S_VS + j)
                    if j >= 2:
                        pe.wait_ge(turn_read, L * 10 + (j - 1))
                turn(L, j, prev)

            def turn_qkv(L, j):
                def prev():
                    wait_read(pe, L, S_QKV + j)
                    if j >= 2:
                        pe.wait_ge(rot_read, L * 5 + (j - 1))
                    else:
                        pe.wait_ge(sgu_read, L * 4 + 4)
                turn(L, 4 + j, prev)

            def turn_rot(L, j):
                pe.wait_ge(roped, L * 5 + (j + 1))
                for t in range(TT):
                    mm = nc.tensor.transpose(aux[:, j % 2, t * P:(t + 1) * P],
                                             rot[:, j % 2, t * P:(t + 1) * P], ident[:])
                mm.then_inc(rot_turned, 1)

            def attention(L):
                def stage(which, it, i):
                    n0 = L * KT + it * 4 + i
                    if which == 0:
                        pe.wait_ge(staged, n0 + 1)
                        if i == 0:
                            pe.wait_ge(rot_read, L * 5 + 5)
                            pe.wait_ge(turn_read, L * 10 + 10)
                        for n in range(4):
                            e, jp = n // 2, n % 2
                            for g in range(2):
                                mm = nc.tensor.matmul(
                                    aux[:, 0, g * HALF + n * P:g * HALF + (n + 1) * P],
                                    qs[g * HD:(g + 1) * HD, e, 2 * jp:2 * jp + 2, :],
                                    ks[g * HD:(g + 1) * HD, e, :], start=True, stop=True)
                        mm.then_inc(scored, 1)
                    elif which == 1:
                        pe.wait_ge(normed, n0 + 1)
                        pe.wait_ge(o_ready, n0 + 1)
                        for n in range(8):
                            mm = nc.tensor.transpose(aux[:, 1, n * P:(n + 1) * P], prob[:, n, :], ident[:])
                        mm.then_inc(p_turned, 1)
                    else:
                        pe.wait_ge(pt_ready, n0 + 1)
                        for e in range(2):
                            for g in range(2):
                                n = 4 * g + 2 * e
                                mm = nc.tensor.matmul(
                                    aux[g * HD:(g + 1) * HD, 1, e * 4 * CHUNK:(e + 1) * 4 * CHUNK],
                                    vst[:, (i % 2) * 2 + e, g * HD:(g + 1) * HD],
                                    probt[:, n:n + 2, :], start=True, stop=True)
                        mm.then_inc(pv_done, 1)
                return stage

            def ones_sum(src, p, done):
                for t in range(2):
                    mm = nc.tensor.matmul(aux[:, p, t * HALF:(t + 1) * HALF], ones[:],
                                          src[:, t * HALF:(t + 1) * HALF], start=True, stop=True)
                mm.then_inc(done, 1)

            def pool_mix_tile(L, j):
                pe.wait_ge(pooled_ready, L * WT + (j + 1))
                if j >= 2:
                    pe.wait_ge(ob_ready, L * WT + (j - 1))
                for t in range(2):
                    mm = nc.tensor.matmul(aux[:, j % 2, t * HALF:(t + 1) * HALF], pmix[:, j, :],
                                          pooled[:, j % 2, t * HALF:(t + 1) * HALF],
                                          start=True, stop=True)
                mm.then_inc(pool_mixed, 1)

            pe.wait_ge(const_loaded, 48)
            pe.wait_ge(consts_made, 1)
            with pe.Fori(0, LAYERS) as L:
                pe.wait_ge(xsq_added, L * KT + KT)
                ones_sum(sumsq, 1, rms_summed)
                projects(L, S_GLU, 8, ready=h_ready)
                for j in range(4):
                    project(L, S_VS + j, between=(lambda j=j: turn_v(L, j - 1)) if j else None)
                for j in range(4):
                    project(L, S_U + j, between=(lambda: turn_v(L, 3)) if j == 0 else None)
                pe.wait_ge(vs_ready, L + 1)
                pe.wait_ge(turn_read, L * 10 + 4)
                for g in range(4):
                    if g >= 2:
                        pe.wait_ge(sgu_read, L * 4 + (g - 1))
                    for n in range(TT):
                        mm = nc.tensor.matmul(aux[:, g % 2, n * P:(n + 1) * P],
                                              vs[:, n, g * P:(g + 1) * P], sgt[:, g, :],
                                              start=True, stop=True)
                    mm.then_inc(sgu_mixed, 1)
                for j in range(6):
                    project(L, S_QKV + j, between=(lambda j=j: turn_qkv(L, j - 1)) if j else None)
                    if j >= 2:
                        turn_rot(L, j - 2)
                for j in range(4):
                    project(L, S_ZC + j, between=(lambda: turn_qkv(L, 5)) if j == 0 else None)
                    if j == 0:
                        turn_rot(L, 4)
                merge(L, S_MC, 1, attention(L))
                projects(L, S_ZA, 4)
                merge(L, S_MA, 2)
                for j in range(4):
                    project(L, S_P + j)
                    if j == 0:
                        pe.wait_ge(mix_loaded, L * 32 + 32)
                        pe.wait_ge(o_ready, L * KT + KT + 1)
                    if j:
                        pool_mix_tile(L, j - 1)
                project(L, S_ZB)
                pool_mix_tile(L, 3)
                for j in range(1, 4):
                    project(L, S_ZB + j)
                merge(L, S_MB, 3)
                pe.wait_ge(conv_summed, L + 1)
                pe.wait_ge(ob_ready, L * 4 + 4)
                ones_sum(sumsq, 0, d_mean)
                project(L, S_ZD)
                project(L, S_ZD + 1)
                pe.wait_ge(d_sumsq, L + 1)
                ones_sum(sumsq, 1, d_var)
                project(L, S_ZD + 2)
                project(L, S_ZD + 3)
                merge(L, S_MD, 4)
                projects(L, S_OUT, 8, ready=mix_ready)

        out_v = out.rearrange("(k p) t -> p k t", p=P)

        @block.scalar
        def _(act):
            def evac(L, s, dst, func, su=0):
                act.wait_ge(unit_used, L * UNITS + UB[s + 1] + su)
                nc.scalar.activation(dst, acc[:, s % 2, :], func).then_inc(acc_read[s % 2], 1)

            def take_z(L, zi, s0, i, it=0):
                act.wait_ge(z_taken, L * 12 + it * 2 + (zi * 4 + i + 1))
                evac(L, s0 + i, EV[(s0 + i) % 2], ACT.Silu, it * 4)

            def gates(L, s0, n_taken):
                if n_taken:
                    act.wait_ge(z_taken, L * 12 + n_taken + 2)
                with act.Fori(0, KT) as d:
                    act.wait_ge(acc_read[1], L * PAIR + d + (s0 // 2 + 1))
                    act.wait_ge(unit_used, L * UNITS + d * 3 + (UB[s0] + 2))
                    nc.scalar.activation(EV[0], acc[:, 0, :], ACT.Sigmoid).then_inc(acc_read[0], 1)

            act.dma_start(out, x).then_inc(x_copied, 16)
            act.sem_inc(acc_read[0], 1)
            act.sem_inc(acc_read[1], 1)
            act.sem_inc(z_taken, 2)
            act.sem_inc(o_ready, 1)
            act.wait_ge(const_loaded, 48)
            act.wait_ge(consts_made, 1)
            act.wait_ge(x_loaded, 16 * KT)
            for k in range(KT):
                if k >= 2:
                    act.wait_ge(xsq_added, k - 1)
                nc.scalar.activation(EV[k % 2], xm[:, k, :], ACT.Square).then_inc(xsq_ready, 1)

            with act.Fori(0, LAYERS) as L:
                nc.scalar.activation(par[:], allp[:].rearrange("p l n -> p (l n)")[:, ds(L * C_N, C_N)],
                                     ACT.Copy).then_inc(par_ready, 1)
                act.wait_ge(rms_summed, L + 1)
                nc.scalar.activation(rstd[:], aux[:, 1, :], ACT.Sqrt, bias=epst[:],
                                     scale=1.0 / D).then_inc(rms_root, 1)
                act.dma_start(rowb[:], rows[ds(L, 1), :].partition_broadcast(P)).then_inc(rows_loaded, 16)
                act.dma_start(sgt[:], sgu_wt[ds(L, 1)]).then_inc(rows_loaded, 16)
                with act.Fori(0, KT // 2) as it:
                    for i in range(2):
                        act.wait_ge(h_scaled, L * KT + it * 2 + (i + 1))
                        settle(act)
                        nc.scalar.activation(hhi[:, ds(it * 2 + i, 1), :], htmp[:, i, :],
                                             ACT.Copy).then_inc(h_hi, 1)
                act.wait_ge(h_ready, L * KT + KT)
                act.dma_start(cosb[:], rope[0]).then_inc(rope_loaded, 16)
                act.dma_start(sinb[:], rope[1]).then_inc(rope_loaded, 16)
                with act.Fori(0, WT) as j:
                    act.wait_ge(acc_read[0], L * PAIR + j + 1)
                    act.wait_ge(unit_used, L * UNITS + j * 4 + 4)
                    nc.scalar.activation(EV[1], acc[:, 1, :], ACT.Sigmoid).then_inc(acc_read[1], 1)
                act.wait_ge(acc_read[0], L * PAIR + (S_VS // 2 + 1))
                for j in range(4):
                    if j >= 2:
                        act.wait_ge(turned, L * 10 + (j - 1))
                    evac(L, S_VS + j, EV[j % 2], ACT.Copy)
                for j in range(4):
                    evac(L, S_U + j, oc[:, j, :], ACT.Copy)
                    if j == 2:
                        act.wait_ge(sgu_var, L + 1)
                        nc.scalar.activation(st[:, 0, :], mv[:, :, 1], ACT.Sqrt,
                                             bias=epst[:]).then_inc(sgu_root, 1)

                def take_turned(j):
                    act.wait_ge(turned, L * 10 + (j + 5))
                    if j == 5:
                        nc.scalar.activation(vt[:], aux[:, 1, :], ACT.Copy).then_inc(turn_read, 1)
                        return
                    if j:
                        act.wait_ge(roped, L * 5 + j)
                    nc.scalar.activation(tok[:], aux[:, j % 2, :], ACT.Copy)
                    nc.scalar.activation(sqt[:], aux[:, j % 2, :], ACT.Square).then_inc(turn_read, 1)
                    act.wait_ge(qk_meansq, L * 5 + (j + 1))
                    nc.scalar.activation(stq[:, 1, :], stq[:, 0, :], ACT.Sqrt, bias=epst[:],
                                         scale=1.0 / HD).then_inc(qk_root, 1)

                def take_rotated(j):
                    act.wait_ge(rot_turned, L * 5 + (j + 1))
                    dst = kt[:] if j == NQT else qo[:, j, :]
                    nc.scalar.activation(dst, aux[:, j % 2, :], ACT.Copy).then_inc(rot_read, 1)

                for j in range(7):
                    if j:
                        take_turned(j - 1)
                    if j < 6:
                        act.wait_ge(turned, L * 10 + (4 if j < 2 else j + 3))
                        evac(L, S_QKV + j, EV[j % 2], ACT.Copy)
                    else:
                        take_z(L, 0, S_ZC, 0)
                    if j >= 2:
                        take_rotated(j - 2)
                for j in range(1, 4):
                    take_z(L, 0, S_ZC, j)

                act.wait_ge(z_taken, L * 12 + (4 + 2))
                act.wait_ge(rot_read, L * 5 + 5)
                act.wait_ge(turn_read, L * 10 + 10)
                with act.Fori(0, 2) as it:
                    for i in range(4):
                        s = S_MC + 2 * i
                        pr = it * (-8) + 15 if i == 0 else it * 8 + (2 * i - 1)
                        pt = it * (-4) + 7 if i == 0 else it * 4 + (i - 1)
                        for e in range(2):
                            c = it * 8 + (2 * i + e)
                            nc.scalar.activation(qs[:, e, :, :], qo[:, :, ds(c * CHUNK, CHUNK)], ACT.Copy)
                        nc.scalar.activation(ks[:, 0, 0:CHUNK],
                                             kt[:, ds(it * (8 * CHUNK) + 2 * i * CHUNK, CHUNK)], ACT.Copy)
                        nc.scalar.activation(ks[:, 0, CHUNK:P], kt[:, ds(pr * CHUNK, CHUNK)], ACT.Copy)
                        nc.scalar.activation(ks[:, 1, :],
                                             kt[:, ds(it * (8 * CHUNK) + 2 * i * CHUNK, P)], ACT.Copy)
                        v0 = (i % 2) * 2
                        nc.scalar.activation(vst[0:CHUNK, v0, :], vt[0:CHUNK, ds(it * 4 + i, 1), :], ACT.Copy)
                        nc.scalar.activation(vst[CHUNK:P, v0, :], vt[CHUNK:P, ds(pt, 1), :], ACT.Copy)
                        nc.scalar.activation(vst[:, v0 + 1, :], vt[:, ds(it * 4 + i, 1), :],
                                             ACT.Copy).then_inc(staged, 1)
                        act.wait_ge(rowmax, L * KT + it * 4 + (i + 1))
                        for n in range(8):
                            nc.scalar.activation(
                                prob[:, n, :], aux[:, 0, n * P:(n + 1) * P], ACT.Exp,
                                bias=st[:, NMAX, n:n + 1], scale=SCALE, accum_out=st[:, PSUM_, n:n + 1])
                        nc.scalar.activation(st[:, ESINK, :], st[:, SDIFF, :], ACT.Exp).then_inc(probs_ready, 1)
                        act.wait_ge(acc_read[1], L * PAIR + it * 4 + (s // 2 + 1))
                        act.wait_ge(unit_used, L * UNITS + it * 12 + (UB[s] + 2))
                        nc.scalar.activation(EV[0], acc[:, 0, :], ACT.Sigmoid).then_inc(acc_read[0], 1)
                wait_read(act, L, S_ZA - 1)
                with act.Fori(0, 2) as it:
                    for i in range(2):
                        take_z(L, 1, S_ZA, i, it)
                gates(L, S_MA, 8)
                act.wait_ge(unit_used, used(L, S_P))
                act.dma_start(pmix[:], pool_mix[ds(L, 1)]).then_inc(mix_loaded, 16)
                act.dma_start(edge[:], edge_in).then_inc(mix_loaded, 16)
                wait_read(act, L, S_P - 1)

                def take_mixed(j):
                    act.wait_ge(pool_mixed, L * WT + (j + 1))
                    nc.scalar.activation(oc[:, j, :], aux[:, j % 2, :], ACT.Copy,
                                         scale=par[:, C_PS + j:C_PS + j + 1]).then_inc(ob_ready, 1)

                for j in range(4):
                    if j >= 2:
                        act.wait_ge(pooled_ready, L * WT + (j - 1))
                    evac(L, S_P + j, EV[j % 2], ACT.Copy)
                    if j:
                        take_mixed(j - 1)
                act.wait_ge(pooled_ready, L * WT + WT)
                take_z(L, 2, S_ZB, 0)
                take_mixed(3)
                for j in range(1, 4):
                    take_z(L, 2, S_ZB, j)
                gates(L, S_MB, 12)
                act.wait_ge(z_taken, L * 12 + (12 + 2))
                wait_read(act, L, S_ZD - 1)
                evac(L, S_ZD, oc[:, 0, :], ACT.Silu)
                for j in range(WT):
                    act.wait_ge(d_centred, L * WT + (j + 1))
                    nc.scalar.activation(csq[:, j, :], conv[:, j, PADC:PADC + SEQ],
                                         ACT.Square).then_inc(d_squared, 1)
                evac(L, S_ZD + 1, oc[:, 1, :], ACT.Silu)
                act.wait_ge(d_var, L + 1)
                nc.scalar.activation(conv[:, WT, PADC:PADC + SEQ], aux[:, 1, :], ACT.Sqrt,
                                     bias=epst[:], scale=1.0 / W).then_inc(d_root, 1)
                evac(L, S_ZD + 2, oc[:, 2, :], ACT.Silu)
                for j in range(WT):
                    act.wait_ge(d_normed, L * WT + (j + 1))
                    nc.scalar.activation(csq[:, j, :], conv[:, j, PADC:PADC + SEQ], ACT.Silu,
                                         bias=par[:, C_CLB + j:C_CLB + j + 1],
                                         scale=par[:, C_CLG + j:C_CLG + j + 1]).then_inc(d_act, 1)
                evac(L, S_ZD + 3, oc[:, 3, :], ACT.Silu)
                act.wait_ge(gated, L * 16 + 16)
                act.wait_ge(x_copied, 16)
                act.dma_start(xin[:], out_v).then_inc(xin_loaded, 16)
                gates(L, S_MD, 0)
                with act.Fori(0, KT) as d:
                    act.wait_ge(merged, L * KT + d + 1)
                    settle(act)
                    nc.scalar.activation(hhi[:, ds(d, 1), :], xm[:, ds(d, 1), :],
                                         ACT.Copy).then_inc(mix_hi, 1)
                with act.Fori(0, KT // 2) as it:
                    for i in range(2):
                        s = S_OUT + i
                        act.wait_ge(acc_read[i], L * PAIR + it + (s // 2 + 2))
                        act.dma_start(out_v[:, ds(it * 2 + i, 1), :],
                                      xm[:, ds(it * 2 + i, 1), :]).then_inc(x_stored, 16)
                        act.wait_ge(xsq_added, L * KT + it * 2 + (KT + i - 1))
                        settle(act)
                        nc.scalar.activation(EV[i], xm[:, ds(it * 2 + i, 1), :],
                                             ACT.Square).then_inc(xsq_ready, 1)
                act.wait_ge(x_stored, L * (16 * KT) + 16 * KT)

        @block.vector
        def _(dve):
            def mul(out, a, b):
                return nc.vector.tensor_tensor(out, a, b, ALU.mult)

            def add(out, a, b):
                return nc.vector.tensor_tensor(out, a, b, ALU.add)

            def gate_tile(L, src, z, j_src, j_dst):
                mul(src[:, ds(j_src, 1), :], z, src[:, ds(j_src, 1), :]).then_inc(z_taken, 1)
                split_tile(src[:, ds(j_src, 1), :], j_dst)

            def split_tile(tile, j):
                dve.drain()
                nc.vector.tensor_copy(bhi[:, ds(j, 1), :], tile)
                dve.drain()
                nc.vector.tensor_tensor(blo[:, ds(j, 1), :], tile, bhi[:, ds(j, 1), :].bitcast(F32),
                                        ALU.subtract).then_inc(gated, 1)

            def gate_loop(L, src, s0):
                with dve.Fori(0, 2) as it:
                    for i in range(2):
                        s = s0 + i
                        dve.wait_ge(acc_read[i], L * PAIR + it + (s // 2 + 2))
                        gate_tile(L, src, EV[i], it * 2 + i, it * 2 + i)

            def merge_tile(L, s0, d, tmp, done=None):
                dve.drain()
                dve.wait_ge(acc_read[0], L * PAIR + d + (s0 // 2 + 2))
                dve.wait_ge(unit_used, L * UNITS + d * 3 + (UB[s0] + 3))
                if tmp is None:
                    mul(xm[:, ds(d, 1), :], EV[0], acc[:, 1, :]).then_inc(acc_read[1], 1)
                    return
                mul(tmp, EV[0], acc[:, 1, :]).then_inc(acc_read[1], 1)
                dve.drain()
                last = add(xm[:, ds(d, 1), :], xm[:, ds(d, 1), :], tmp)
                if done is not None:
                    last.then_inc(done, 1)

            convf = conv[:].rearrange("p s t -> p (s t)")
            SW = PADC + SEQ

            def conv_merge(L, s0, j0):
                with dve.Fori(0, 2) as it:
                    for i in range(4):
                        o = convf[:, ds(it * SW + (j0 * SW + PADC), SEQ)]
                        for k in range(8 * i, min(8 * i + 8, TAPS)):
                            h = convf[:, ds(it * SW + ((j0 + 1) * SW + PADC - (TAPS - 1) + k), SEQ)]
                            w = par[:, ds(it * TAPS + (C_CW + j0 * TAPS + k), 1)]
                            if k == 0:
                                nc.vector.tensor_scalar(o, h, w, par[:, ds(it + (C_CB + j0), 1)],
                                                        ALU.mult, ALU.add)
                            else:
                                nc.vector.scalar_tensor_tensor(out=o, in0=h, scalar=w, in1=o,
                                                               op0=ALU.mult, op1=ALU.add)
                            dve.drain()
                        merge_tile(L, s0, it * 4 + i, oc[:, 0, :])

            for t in (ev[:, :, 0:POOL_PAD], conv[:, :, 0:PADC], sumsq[:]):
                nc.vector.memset(t, 0.0)
            nc.vector.memset(ones[:], 1.0)
            nc.vector.memset(epst[:], EPS)
            dve.drain()
            nc.vector.memset(st[:], 0.0).then_inc(consts_made, 1)
            for k in range(KT):
                dve.wait_ge(xsq_ready, k + 1)
                add(sumsq[:], sumsq[:], EV[k % 2]).then_inc(xsq_added, 1)
                dve.drain()

            with dve.Fori(0, LAYERS) as L:
                dve.wait_ge(par_ready, L + 1)
                nc.vector.tensor_scalar(nsink[:], par[:, C_SINK:C_SINK + 8], -1.0, None, ALU.mult)
                dve.wait_ge(rms_root, L + 1)
                nc.vector.reciprocal(rstd[:], rstd[:])
                dve.drain()
                with dve.Fori(0, KT // 2) as it:
                    dve.drain()
                    for i in range(2):
                        nc.vector.scalar_tensor_tensor(
                            out=htmp[:, i, :], in0=xm[:, ds(it * 2 + i, 1), :],
                            scalar=par[:, ds(it * 2 + (C_G + i), 1)], in1=rstd[:], op0=ALU.mult,
                            op1=ALU.mult).then_inc(h_scaled, 1)
                    for i in range(2):
                        dve.wait_ge(h_hi, L * KT + it * 2 + (i + 1))
                        nc.vector.tensor_tensor(hlo[:, ds(it * 2 + i, 1), :], htmp[:, i, :],
                                                hhi[:, ds(it * 2 + i, 1), :].bitcast(F32),
                                                ALU.subtract).then_inc(h_ready, 1)
                with dve.Fori(0, WT) as j:
                    dve.wait_ge(acc_read[1], L * PAIR + j + 2)
                    mul(convf[:, ds(j * SW + (SW + PADC), SEQ)], acc[:, 0, :],
                        EV[1]).then_inc(acc_read[0], 1)
                for j in range(4):
                    dve.wait_ge(turned, L * 10 + (j + 1))
                    nc.vector.tensor_copy(vs[:, :, j * P:(j + 1) * P],
                                          aux[:, j % 2, :].rearrange("p (t c) -> p t c", c=P)
                                          ).then_inc(turn_read, 1)
                dve.drain()
                for t in range(TT):
                    nc.vector.bn_stats(stv[:, t, :], vs[:, t, :])
                dve.drain()
                for t in range(TT):
                    last = nc.vector.bn_aggr(mv[:, t, :], stv[:, t, :])
                last.then_inc(sgu_var, 1)
                dve.wait_ge(rows_loaded, L * 32 + 32)
                nc.vector.memset(sgt[CHUNK:P, :, 0:CHUNK], 0.0)
                dve.wait_ge(rope_loaded, L * 32 + 32)
                for q in range(2):
                    for n, (t, half) in enumerate(((cosb, 0), (sinb, 1), (cosb, 1), (sinb, 0))):
                        g0 = R_QK + q * HD + half * (HD // 2)
                        g = rowb[:, g0:g0 + HD // 2].unsqueeze(1).to_broadcast([P, TT, HD // 2])
                        mul(ropeb[:, q, n, :, :], t[:], g)
                dve.wait_ge(sgu_root, L + 1)
                nc.vector.reciprocal(st[:, 1, :], st[:, 0, :])
                dve.drain()
                for t in range(TT):
                    nc.vector.tensor_scalar(vs[:, t, :], vs[:, t, :], mv[:, t, 0:1], st[:, 1, t:t + 1],
                                            ALU.subtract, ALU.mult)
                dve.drain()
                mul(vs[:], vs[:], rowb[:, R_G:R_G + W].unsqueeze(1).to_broadcast([P, TT, W]))
                dve.drain()
                add(vs[:], vs[:], rowb[:, R_B:R_B + W].unsqueeze(1).to_broadcast([P, TT, W])
                    ).then_inc(vs_ready, 1)
                wait_read(dve, L, S_U + 2)
                wait_read(dve, L, S_U + 3)
                for g in range(4):
                    dve.wait_ge(sgu_mixed, L * 4 + (g + 1))
                    bs = rowb[:, R_BS + g * P:R_BS + (g + 1) * P].unsqueeze(1).to_broadcast([P, TT, P])
                    add(stmp[:].rearrange("p (n i) -> p n i", i=P),
                        aux[:, g % 2, :].rearrange("p (n i) -> p n i", i=P), bs).then_inc(sgu_read, 1)
                    dve.drain()
                    mul(oc[:, g, :], stmp[:], oc[:, g, :])
                    dve.drain()
                v4 = tok[:].rearrange("p (t h a d) -> p t h a d", t=TT, h=2, a=2)
                f1 = rt1[:].rearrange("p (t h d) -> p t h d", t=TT, h=2)
                f2 = rt2[:].rearrange("p (t h d) -> p t h d", t=TT, h=2)
                for j in range(5):
                    dve.drain()
                    tab = [ropeb[:, j // NQT, n, :, :].unsqueeze(2).to_broadcast([P, TT, 2, HD // 2])
                           for n in range(4)]
                    r4 = rot[:, j % 2, :].rearrange("p (t h a d) -> p t h a d", t=TT, h=2, a=2)
                    dve.wait_ge(turn_read, L * 10 + (j + 5))
                    nc.vector.tensor_reduce(stq[:, 0, :], sqt[:].rearrange("p (n d) -> p n d", d=HD),
                                            AX.X, ALU.add).then_inc(qk_meansq, 1)
                    dve.wait_ge(qk_root, L * 5 + (j + 1))
                    nc.vector.reciprocal(stq[:, 1, :], stq[:, 1, :])
                    dve.drain()
                    tn = tok[:].rearrange("p (n d) -> p n d", d=HD)
                    mul(tn, tn, stq[:, 1, :].unsqueeze(2).to_broadcast([P, NPAIRS, HD]))
                    dve.drain()
                    if j >= 2:
                        dve.wait_ge(rot_turned, L * 5 + (j - 1))
                    mul(f1, v4[:, :, :, 0, :], tab[0])
                    mul(f2, v4[:, :, :, 1, :], tab[1])
                    dve.drain()
                    nc.vector.tensor_tensor(r4[:, :, :, 0, :], f1, f2, ALU.subtract)
                    dve.drain()
                    mul(f1, v4[:, :, :, 1, :], tab[2])
                    mul(f2, v4[:, :, :, 0, :], tab[3])
                    dve.drain()
                    add(r4[:, :, :, 1, :], f1, f2).then_inc(roped, 1)
                gate_loop(L, oc, S_ZC)

                with dve.Fori(0, 2) as it:
                    for i in range(4):
                        n0 = L * KT + it * 4 + i
                        dve.wait_ge(scored, n0 + 1)
                        sc = aux[:, 0, :].rearrange("p (n k) -> p n k", k=P)
                        if i == 0:
                            m = mask[:, ds(it, 1), :].to_broadcast([P, 2, CHUNK])
                            for g in range(2):
                                s0 = sc[:, 4 * g:4 * g + 2, CHUNK:P]
                                add(s0, s0, m)
                            dve.drain()
                        nc.vector.tensor_reduce(st[:, MAXS, :], sc, AX.X, ALU.max)
                        dve.drain()
                        nc.vector.scalar_tensor_tensor(
                            out=st[:, NMAX, :], in0=st[:, MAXS, :], scalar=-SCALE,
                            in1=nsink[:], op0=ALU.mult, op1=ALU.min)
                        dve.drain()
                        nc.vector.tensor_tensor(st[:, SDIFF, :], st[:, NMAX, :], nsink[:],
                                                ALU.subtract).then_inc(rowmax, 1)
                        dve.wait_ge(probs_ready, n0 + 1)
                        add(st[:, DEN, :], st[:, PSUM_, :], st[:, ESINK, :])
                        dve.drain()
                        nc.vector.reciprocal(st[:, RDEN, :], st[:, DEN, :])
                        dve.drain()
                        mul(prob[:], prob[:],
                            st[:, RDEN, :].unsqueeze(2).to_broadcast([P, 8, P])).then_inc(normed, 1)
                        dve.wait_ge(p_turned, n0 + 1)
                        nc.vector.tensor_copy(probt[:].rearrange("p n q -> p (n q)"),
                                              aux[:, 1, :]).then_inc(pt_ready, 1)
                        dve.wait_ge(pv_done, n0 + 1)
                        nc.vector.tensor_copy(
                            qo[:, :, ds((it * 4 + i) * P, P)].rearrange("p n (e q) -> p e n q", e=2),
                            aux[:, 1, 0:8 * CHUNK].rearrange("p (e n q) -> p e n q", e=2, n=4)
                        ).then_inc(o_ready, 1)
                        merge_tile(L, S_MC, it * 4 + i, None)
                dve.drain()
                gate_loop(L, qo, S_ZA)
                conv_merge(L, S_MA, 0)

                dve.wait_ge(mix_loaded, L * 32 + 32)
                nc.vector.memset(pool1[:, 0:POOL_PAD], 0.0)
                nc.vector.memset(pool2[:, 0:POOL_PAD], 0.0)
                dve.drain()
                for j, w in enumerate(POOL_W):
                    dve.drain()
                    wait_read(dve, L, S_P + j)
                    src = ev[:, j % 2, :]
                    shift = 1
                    bufs = [pool1, pool2]
                    while shift < w:
                        if shift > 1:
                            dve.drain()
                        dst = bufs.pop(0)
                        bufs.append(dst)
                        add(dst[:, POOL_PAD:], src[:, POOL_PAD:],
                            src[:, POOL_PAD - shift:POOL_PAD - shift + SEQ])
                        src, shift = dst, 2 * shift
                    dve.drain()
                    if j >= 2:
                        dve.wait_ge(pool_mixed, L * WT + (j - 1))
                    nc.vector.scalar_tensor_tensor(out=pooled[:, j % 2, :], in0=src[:, POOL_PAD:],
                                                   scalar=1.0 / w, in1=EV[j % 2], op0=ALU.mult,
                                                   op1=ALU.subtract)
                    dve.drain()
                    mul(pooled[:, j % 2, 0:POOL_PAD], src[:, POOL_PAD:2 * POOL_PAD], edge[:, j, :])
                    dve.drain()
                    nc.vector.tensor_tensor(pooled[:, j % 2, 0:POOL_PAD], pooled[:, j % 2, 0:POOL_PAD],
                                            EV[j % 2][:, 0:POOL_PAD], ALU.subtract).then_inc(pooled_ready, 1)
                dve.wait_ge(ob_ready, L * WT + WT)
                settle(dve)
                gate_loop(L, oc, S_ZB)
                conv_merge(L, S_MB, 2)

                cv = [conv[:, j, PADC:SW] for j in range(WT + 1)]
                dve.drain()
                add(sumsq[:], cv[0], cv[1])
                dve.drain()
                add(sumsq[:], sumsq[:], cv[2])
                dve.drain()
                add(sumsq[:], sumsq[:], cv[3]).then_inc(conv_summed, 1)
                dve.wait_ge(d_mean, L + 1)
                for j in range(WT):
                    nc.vector.scalar_tensor_tensor(out=cv[j], in0=aux[:, 0, :], scalar=-1.0 / W,
                                                   in1=cv[j], op0=ALU.mult,
                                                   op1=ALU.add).then_inc(d_centred, 1)
                dve.wait_ge(d_squared, L * WT + 2)
                add(sumsq[:], csq[:, 0, :], csq[:, 1, :])
                dve.drain()
                dve.wait_ge(d_squared, L * WT + 3)
                add(sumsq[:], sumsq[:], csq[:, 2, :])
                dve.drain()
                dve.wait_ge(d_squared, L * WT + 4)
                add(sumsq[:], sumsq[:], csq[:, 3, :]).then_inc(d_sumsq, 1)
                dve.wait_ge(d_root, L + 1)
                nc.vector.reciprocal(cv[WT], cv[WT])
                dve.drain()
                for j in range(WT):
                    mul(cv[j], cv[j], cv[WT]).then_inc(d_normed, 1)
                nc.vector.memset(sumsq[:], 0.0)
                dve.wait_ge(unit_used, used(L, S_ZD))
                for j in range(WT):
                    wait_read(dve, L, S_ZD + j)
                    dve.wait_ge(d_act, L * WT + (j + 1))
                    mul(csq[:, j, :], csq[:, j, :], oc[:, j, :])
                    split_tile(csq[:, j:j + 1, :], j)
                with dve.Fori(0, KT) as d:
                    merge_tile(L, S_MD, d, cv[WT], merged)
                with dve.Fori(0, KT) as d:
                    dve.wait_ge(mix_hi, L * KT + d + 1)
                    nc.vector.tensor_tensor(hlo[:, ds(d, 1), :], xm[:, ds(d, 1), :],
                                            hhi[:, ds(d, 1), :].bitcast(F32),
                                            ALU.subtract).then_inc(mix_ready, 1)
                dve.wait_ge(xin_loaded, L * 16 + 16)
                settle(dve)
                with dve.Fori(0, KT // 2) as it:
                    for i in range(2):
                        s = S_OUT + i
                        dve.wait_ge(unit_used, L * UNITS + it * 4 + UB[s + 1])
                        add(xm[:, ds(it * 2 + i, 1), :], acc[:, i, :],
                            xin[:, ds(it * 2 + i, 1), :]).then_inc(acc_read[i], 1)
                        dve.wait_ge(xsq_ready, L * KT + it * 2 + (KT + i + 1))
                        add(sumsq[:], sumsq[:], EV[i]).then_inc(xsq_added, 1)
                        dve.drain()


def column_tiles():
    names = ["q", "k", "v", "za", "p", "zb", "u", "vs", "zc", "ga", "gb", "zd"]
    sizes = [W, P, P, W, W, W, W, W, W, W, W, W]
    at = dict(zip(names, [sum(sizes[:i]) for i in range(len(sizes))]))
    return at, sum(sizes)


def kernel(**inputs):
    import numpy as np
    import concourse.bacc as bacc
    from concourse.bass_utils import run_bass_kernel_spmd

    a = {k: np.asarray(v) for k, v in inputs.items()}
    at, merge0 = column_tiles()

    def pair_cols(base, j):
        return np.concatenate([np.arange(base + j * HD, base + (j + 1) * HD),
                               np.arange(base + (j + 4) * HD, base + (j + 5) * HD)])

    def plain(base, j):
        return np.arange(base + j * P, base + (j + 1) * P)

    def units(w):
        k = w.shape[0] // W
        return w.reshape(k, UK, P, P).transpose(0, 2, 1, 3).reshape(k, P, UW)

    perm = np.concatenate([pair_cols(0, j) for j in range(4)])
    stream = []
    for l in range(LAYERS):
        w_in, w_br, w_out = a["w_in"][l], a["w_branch"][l], a["w_out"][l]

        def proj(cols):
            stream.append(units(w_in[:, cols]))

        def merge(n):
            wb = w_br[n][perm] if n == 0 else w_br[n]
            for d in range(KT):
                proj(plain(merge0 + n * D, d))
                stream.append(units(wb[:, d * P:(d + 1) * P]))

        for j in range(4):
            proj(plain(at["ga"], j))
            proj(plain(at["gb"], j))
        for n in ("vs", "u"):
            for j in range(4):
                proj(plain(at[n], j))
        for j in range(4):
            proj(pair_cols(at["q"], j))
        proj(plain(at["k"], 0))
        proj(plain(at["v"], 0))
        for j in range(4):
            proj(plain(at["zc"], j))
        merge(2)
        for j in range(4):
            proj(pair_cols(at["za"], j))
        merge(0)
        for n in ("p", "zb"):
            for j in range(4):
                proj(plain(at[n], j))
        merge(1)
        for j in range(4):
            proj(plain(at["zd"], j))
        merge(3)
        for d in range(KT):
            stream.append(units(w_out[:, d * P:(d + 1) * P]))
    wstream = np.ascontiguousarray(np.concatenate(stream))
    assert wstream.shape[0] == LAYERS * UNITS

    def tiles(v):
        return np.moveaxis(v.reshape(*v.shape[:-1], -1, P), -1, 0)

    cols = []
    for l in range(LAYERS):
        cw = a["conv_w"][l]
        cwt = cw.reshape(TAPS, WT, P).transpose(2, 1, 0).reshape(P, WT * TAPS)
        sk = a["attn_sinks"][l].reshape(2, 2, 2)
        sink = np.broadcast_to(sk.transpose(2, 0, 1)[:, :, None, :], (2, 2, 2, 2)).reshape(2, 8)
        sink = np.repeat(sink, CHUNK, axis=0)
        cols.append(np.concatenate([tiles(a["norm_g"][l]), cwt, tiles(a["conv_b"][l]),
                                    tiles(a["conv_ln_g"][l]), tiles(a["conv_ln_b"][l]),
                                    tiles(a["pool_scale"][l]), sink], axis=1))
    cols = np.ascontiguousarray(np.stack(cols, 1))
    rows = np.ascontiguousarray(np.concatenate(
        [a["sgu_ln_g"], a["sgu_ln_b"], a["sgu_b"].reshape(LAYERS, W), a["q_norm_g"], a["k_norm_g"]], 1))
    sgu_wt = np.ascontiguousarray(a["sgu_w"].transpose(0, 3, 1, 2))
    pool_mix = np.ascontiguousarray(a["pool_mix"].transpose(0, 2, 1, 3))
    pos = np.arange(SEQ, dtype=np.float32)
    inv = (1.0 / (np.float32(10000.0) ** (np.arange(0, HD, 2, dtype=np.float32) / np.float32(HD)))
           ).astype(np.float32)
    ang = (pos[:, None] * inv[None, :]).astype(np.float32).astype(np.float64)
    rope = np.ascontiguousarray(np.stack([
        t.astype(np.float32).reshape(TT, P, HD // 2).transpose(1, 0, 2)
        for t in (np.cos(ang), np.sin(ang))]))
    ident = np.eye(P, dtype=np.float32)
    mask = np.zeros((P, 2, CHUNK), np.float32)
    mask[:, 0] = NEG
    edge = np.stack([1.0 / np.minimum(np.arange(1, POOL_PAD + 1), w) for w in POOL_W]).astype(np.float32)
    edge = np.ascontiguousarray(np.broadcast_to(edge, (P, WT, POOL_PAD)))

    arrays = {"x": np.ascontiguousarray(a["x"][0].T), "wstream": wstream, "cols": cols, "rows": rows,
              "sgu_wt": sgu_wt, "pool_mix": pool_mix, "rope": rope, "ident": ident, "mask_in": mask,
              "edge_in": edge}
    nc = bacc.Bacc("TRN2", target_bir_lowering=False, num_devices=1, dynamic_dma_scratch_size=1024)
    args = [nc.dram_tensor(k, v.shape, mybir.dt.from_np(v.dtype), kind="ExternalInput").ap()
            for k, v in arrays.items()]
    res = nc.dram_tensor("out", (D, SEQ), F32, kind="ExternalOutput").ap()
    hybrid_block(nc, *args, res)
    r = run_bass_kernel_spmd(nc, [arrays], core_ids=[0])
    return np.ascontiguousarray(r.results[0]["out"].T)[None]
```

```python
from contextlib import ExitStack

import concourse.bass as bass
from concourse import mybir
from concourse.alu_op_type import AluOpType as ALU

F32 = mybir.dt.float32
F32R = mybir.dt.float32r
ACT = mybir.ActivationFunctionType
AX = mybir.AxisListType
ds = bass.ds

P = 128
LAYERS = 2
D = 1024
SEQ = 1024
W = 512
HD = 64
CHUNK = 64
NCHUNK = SEQ // CHUNK
KT = D // P
WT = W // P
TT = SEQ // P
HALF = 512
NQT = 4
NPAIRS = TT * 2
TAPS = 31
PADC = TAPS + 1
POOL_W = (2, 4, 8, 16)
POOL_PAD = 16
H_TILES = [(), (0, 1), (2, 3), (4, 5), (6, 7), (), (), ()]
EPS = 1e-6
SCALE = HD ** -0.5
NEG = -1e30

S_GLU, S_VS, S_U, S_QKV, S_ZC, S_MC, S_ZA, S_MA, S_P, S_ZB, S_MB, S_ZD, S_MD, S_OUT, STEPS = (
    0, 8, 12, 16, 22, 26, 42, 46, 62, 66, 70, 86, 90, 106, 122)
PAIR = STEPS // 2


def unit_bases():
    at, out = 0, {}
    for s in range(STEPS + 1):
        out[s] = at
        merge = any(a <= s < a + 16 for a in (S_MC, S_MA, S_MB, S_MD))
        at += 1 if merge and (s - S_MC) % 2 else 2
    return out


UB = unit_bases()
UNITS = UB[STEPS]
UK = 4
UW = UK * P
SLOTS = 4
RAWS = 2
WARMUP = 16
HTMP = 4

C_G = 0
C_CW = C_G + KT
C_CB = C_CW + WT * TAPS
C_CLG = C_CB + WT
C_CLB = C_CLG + WT
C_PS = C_CLB + WT
C_SINK = C_PS + WT
C_N = C_SINK + 8
MAXS, NMAX, SDIFF, PSUM_, ESINK, DEN, RDEN = range(7)
R_G, R_B, R_BS, R_QK, R_N = 0, W, 2 * W, 3 * W, 3 * W + 2 * HD


def hybrid_block(nc, x, wstream, cols, rows, sgu_wt, pool_mix, rope, ident_in, mask_in, edge_in, out):
    ctx = ExitStack()
    with ctx:
        cursor = [(nc.sbuf_base + 63) // 64 * 64]

        def place(name, shape, dt, at=None):
            n = 4
            for v in shape[1:]:
                n *= v
            if at is None:
                at = cursor[0]
                cursor[0] = at + (n + 63) // 64 * 64
                assert cursor[0] <= nc.sbuf_usable_end, (name, cursor[0], nc.sbuf_usable_end)
            return nc.alloc_sbuf_tensor_at(name, shape, dt, offset=at)

        def sem(name):
            return ctx.enter_context(nc.semaphore(name))

        hhi = place("hhi", [P, KT, SEQ], F32R)
        hlo = place("hlo", [P, KT, SEQ], F32R)
        at_x = cursor[0]
        xm = place("xm", [P, KT, SEQ], F32)
        cosb = place("cosb", [P, TT, HD // 2], F32, at_x)
        sinb = place("sinb", [P, TT, HD // 2], F32, at_x + 1024)
        ropeb = place("ropeb", [P, 2, 4, TT, HD // 2], F32, at_x + 2048)
        tok = place("tok", [P, SEQ], F32, at_x + 10240)
        sqt = place("sqt", [P, SEQ], F32, at_x + 14336)
        rot = place("rot", [P, 2, SEQ], F32, at_x + 18432)
        rt1 = place("rt1", [P, W], F32, at_x + 26624)
        rt2 = place("rt2", [P, W], F32, at_x + 28672)
        at_b = cursor[0]
        bhi = place("bhi", [P, WT, SEQ], F32R)
        blo = place("blo", [P, WT, SEQ], F32R)
        rowb = place("rowb", [P, R_N], F32, at_b)
        sgt = place("sgt", [P, WT, P], F32, at_b + 7168)
        stmp = place("stmp", [P, SEQ], F32, at_b + 9216)
        diag = place("diag", [P, TT // 2, P], F32, at_b + 13312)
        htmp = place("htmp", [P, HTMP, HALF], F32, at_b + 15360)
        pmix = place("pmix", [P, WT, P], F32, at_b)
        edge = place("edge", [P, WT, POOL_PAD], F32, at_b + 2048)
        pool1 = place("pool1", [P, POOL_PAD + SEQ], F32, at_b + 2560)
        pool2 = place("pool2", [P, POOL_PAD + SEQ], F32, at_b + 2560 + 4160)
        pooled = place("pooled", [P, 2, SEQ], F32, at_b + 2560 + 8320)
        raw = place("raw", [P, RAWS, UW], F32)
        whi = place("whi", [P, SLOTS, UW], F32R)
        wlo = place("wlo", [P, SLOTS, UW], F32R)
        at_conv = cursor[0]
        conv = place("conv", [P, WT + 1, PADC + SEQ], F32)
        at_r2 = cursor[0]
        vs = place("vs", [P, TT, W], F32)
        qo = place("qo", [P, NQT, SEQ], F32, at_r2)
        csq = place("csq", [P, WT, SEQ], F32, at_r2)
        at_r3 = cursor[0]
        oc = place("oc", [P, WT, SEQ], F32)
        kt = place("kt", [P, SEQ], F32, at_conv)
        vt = place("vt", [P, TT, P], F32)
        xin = place("xin", [P, KT, SEQ], F32, at_r2)
        assert at_r3 == at_r2 + 16384
        ev = place("ev", [P, 2, POOL_PAD + SEQ], F32)
        EV = [ev[:, p, POOL_PAD:POOL_PAD + SEQ] for p in range(2)]
        at_sums = cursor[0]
        sumsq = place("sumsq", [P, SEQ], F32)
        qs = place("qs", [P, 2, NQT, CHUNK], F32, at_sums)
        ks = place("ks", [P, 2, P], F32, at_sums + 2048)
        vst = place("vst", [P, 4, P], F32, at_r3 + 3072)
        prob = place("prob", [P, 8, P], F32, at_r3 + 5120)
        probt = place("probt", [P, 8, P], F32, at_r3 + 9216)
        st = place("st", [P, 8, 8], F32)
        stq = place("stq", [P, 2, NPAIRS], F32)
        stv = place("stv", [P, TT, 6], F32)
        mv = place("mv", [P, TT, 2], F32)
        allp = place("allp", [P, LAYERS + 1, C_N], F32)
        par = place("par", [P, C_N], F32)
        rms = place("rms", [P, TT // 2], F32)
        nsink = place("nsink", [P, 8], F32)
        epst = place("epst", [P, 1], F32)
        ones = place("ones", [P, P], F32)
        ident = place("ident", [P, P], F32)
        mask = place("mask", [P, 2, CHUNK], F32)

        acc = ctx.enter_context(nc.psum_tensor("acc", [P, 2, SEQ], F32))
        aux = ctx.enter_context(nc.psum_tensor("aux", [P, 2, SEQ], F32))

        const_loaded = sem("const_loaded")
        x_loaded = [sem(f"x_loaded{i}") for i in range(KT)]
        x_copied = sem("x_copied")
        rows_loaded = sem("rows_loaded")
        mix_loaded = sem("mix_loaded")
        xin_loaded = sem("xin_loaded")
        x_stored = sem("x_stored")
        raw_loaded = [sem(f"raw_loaded{i}") for i in range(RAWS)]
        hi_split = sem("hi_split")
        unit_split = sem("unit_split")
        unit_used = sem("unit_used")
        acc_read = [sem(f"acc_read{p}") for p in range(2)]
        consts_made = sem("consts_made")
        par_ready = sem("par_ready")
        tok_summed = sem("tok_summed")
        rms_root = sem("rms_root")
        rms_diag = sem("rms_diag")
        rms_spread = sem("rms_spread")
        h_scaled = sem("h_scaled")
        h_hi = sem("h_hi")
        h_ready = sem("h_ready")
        turned = sem("turned")
        turn_read = sem("turn_read")
        sgu_var = sem("sgu_var")
        sgu_root = sem("sgu_root")
        vs_ready = sem("vs_ready")
        sgu_mixed = sem("sgu_mixed")
        sgu_read = sem("sgu_read")
        z_taken = sem("z_taken")
        gated = sem("gated")
        qk_meansq = sem("qk_meansq")
        qk_root = sem("qk_root")
        roped = sem("roped")
        rot_turned = sem("rot_turned")
        rot_read = sem("rot_read")
        staged = sem("staged")
        scored = sem("scored")
        rowmax = sem("rowmax")
        probs_ready = sem("probs_ready")
        normed = sem("normed")
        p_turned = sem("p_turned")
        pt_ready = sem("pt_ready")
        pv_done = sem("pv_done")
        o_ready = sem("o_ready")
        pooled_ready = sem("pooled_ready")
        pool_mixed = sem("pool_mixed")
        ob_ready = sem("ob_ready")
        conv_summed = sem("conv_summed")
        d_mean = sem("d_mean")
        d_centred = sem("d_centred")
        d_squared = sem("d_squared")
        d_sumsq = sem("d_sumsq")
        d_var = sem("d_var")
        d_root = sem("d_root")
        d_normed = sem("d_normed")
        d_act = sem("d_act")
        merged = sem("merged")
        mix_hi = sem("mix_hi")
        mix_ready = sem("mix_ready")
        x_summed = sem("x_summed")
        xsq_ready = sem("xsq_ready")
        xsq_added = sem("xsq_added")
        rope_loaded = sem("rope_loaded")

        settled = sem("settled")

        block = ctx.enter_context(nc.Block())

        def used(L, s, k=0):
            return L * UNITS + (UB[s] + k)

        def settle(eng):
            eng.sem_inc(settled, 1)

        def wait_read(eng, L, s, more=0):
            eng.wait_ge(acc_read[s % 2], L * PAIR + more + (s // 2 + 2))

        @block.sync
        def _(sp):
            for n in range(2 * KT):
                t, k = n // KT, n % KT
                sp.dma_start(xm[:, k, t * HALF:(t + 1) * HALF],
                             x[k * P:(k + 1) * P, t * HALF:(t + 1) * HALF]).then_inc(x_loaded[n // 2], 16)
                if n == KT - 1:
                    for t, src in ((ident, ident_in), (allp, cols), (mask, mask_in)):
                        sp.dma_start(t[:], src).then_inc(const_loaded, 16)
                    sp.dma_start(raw[:, 0, :], wstream[0]).then_inc(raw_loaded[0], 16)
            sp.dma_start(raw[:, 1, :], wstream[1]).then_inc(raw_loaded[1], 16)
            with sp.Fori(1, LAYERS * UNITS // RAWS) as b:
                for i in range(RAWS):
                    sp.wait_ge(unit_split, b * RAWS + (i - RAWS + 1))
                    sp.dma_start(raw[:, i, :], wstream[b * RAWS + i]).then_inc(raw_loaded[i], 16)

        @block.gpsimd
        def _(pool):
            def split(i, loads, n, first):
                pool.wait_ge(raw_loaded[i % RAWS], loads * 16)
                if not first:
                    pool.wait_ge(unit_used, n - (SLOTS - 1))
                    settle(pool)
                nc.gpsimd.tensor_scalar(whi[:, i, :], raw[:, i % RAWS, :], 1.0, 0.0, ALU.mult,
                                        ALU.add).then_inc(hi_split, 1)
                pool.wait_ge(hi_split, n + 1)
                nc.gpsimd.tensor_tensor(wlo[:, i, :], raw[:, i % RAWS, :],
                                        whi[:, i, :].bitcast(F32), ALU.subtract).then_inc(unit_split, 1)

            for i in range(SLOTS):
                split(i, i // RAWS + 1, i, True)
            with pool.Fori(1, LAYERS * UNITS // SLOTS) as b:
                for i in range(SLOTS):
                    split(i, b * (SLOTS // RAWS) + (i // RAWS + 1), b * SLOTS + i, False)

        @block.tensor
        def _(pe):
            def unit(L, u, slot, kbase, p, src, first, last, halves=(0, 1), done=1):
                hi, lo = src
                pe.wait_ge(unit_split, L * UNITS + u + 1)
                for k in range(UK):
                    wh = whi[:, slot, k * P:(k + 1) * P]
                    wl = wlo[:, slot, k * P:(k + 1) * P]
                    for n, (w, m) in enumerate(((wh, hi), (wh, lo), (wl, hi))):
                        for t in halves:
                            mm = nc.tensor.matmul(
                                acc[:, p, t * HALF:(t + 1) * HALF], w,
                                m[:, kbase + k, t * HALF:(t + 1) * HALF],
                                start=first and k == 0 and n == 0,
                                stop=last and k == UK - 1 and n == 2)
                if done:
                    mm.then_inc(unit_used, done)

            H = (hhi, hlo)
            B = (bhi, blo)

            def project(L, s, between=None, su=0, sr=0, halves=(0, 1), mixed=None):
                p = s % 2
                pe.wait_ge(acc_read[p], L * PAIR + sr + (s // 2 + 1))
                if mixed is not None:
                    pe.wait_ge(mix_ready, L * 2 * KT + (mixed * KT + UK))
                unit(L, UB[s] + su, UB[s] % SLOTS, 0, p, H, True, False, halves)
                if between:
                    between()
                if mixed is not None:
                    pe.wait_ge(mix_ready, L * 2 * KT + (mixed * KT + KT))
                unit(L, UB[s] + 1 + su, (UB[s] + 1) % SLOTS, UK, p, H, False, True, halves)

            def projects(L, s0, n, halves=(0, 1), mixed=None):
                with pe.Fori(0, n // 2) as it:
                    for i in range(2):
                        project(L, s0 + i, None, it * 4, it, halves, mixed)

            def first_tiles(L):
                for n in range(4):
                    p, k = n // 2, n % 2
                    if k == 0:
                        pe.wait_ge(acc_read[p], L * PAIR + 1)
                    pe.wait_ge(h_ready, L * 2 * KT + (k + 1) * UK)
                    unit(L, n, n, k * UK, p, H, k == 0, k == 1, (0,), 0)
                    if n < 2:
                        (token_sums, spread)[n](L * 2 + 1, 1)
                for n, count in ((0, 1), (2, 0), (1, 2), (3, 1)):
                    p, k = n // 2, n % 2
                    pe.wait_ge(h_ready, L * 2 * KT + (KT + (k + 1) * UK))
                    unit(L, n, n, k * UK, p, H, k == 0, k == 1, (1,), count)

            def token_sums(stage, t):
                pe.wait_ge(xsq_added, stage * KT + KT)
                for n in range(TT // 2):
                    mm = nc.tensor.matmul(aux[:, 0, n:n + 1], sumsq[:, t * HALF + n * P:t * HALF + (n + 1) * P],
                                          ones[:, 0:1], start=True, stop=True)
                mm.then_inc(tok_summed, 1)

            def spread(stage, t):
                pe.wait_ge(rms_diag, stage + 1)
                nc.tensor.matmul(aux[:, 1, t * HALF:(t + 1) * HALF], ones[:],
                                 diag[:].rearrange("p n c -> p (n c)"),
                                 start=True, stop=True).then_inc(rms_spread, 1)

            def merge(L, s0, nb, attention=None):
                with pe.Fori(0, 2) as it:
                    for i in range(4):
                        s = s0 + 2 * i
                        if attention:
                            attention(0, it, i)
                        project(L, s, None, it * 12, it * 4)
                        if attention:
                            attention(1, it, i)
                        pe.wait_ge(gated, L * 16 + 4 * nb)
                        pe.wait_ge(acc_read[1], L * PAIR + it * 4 + (s // 2 + 1))
                        unit(L, UB[s + 1] + it * 12, UB[s + 1] % SLOTS, 0, 1, B, True, True)
                        if attention:
                            attention(2, it, i)

            def turn(L, n, prev):
                p = n % 2
                prev()
                for t in range(TT):
                    mm = nc.tensor.transpose(aux[:, p, t * P:(t + 1) * P],
                                             EV[p][:, t * P:(t + 1) * P], ident[:])
                mm.then_inc(turned, 1)

            def turn_v(L, j):
                def prev():
                    wait_read(pe, L, S_VS + j)
                    if j >= 2:
                        pe.wait_ge(turn_read, L * 10 + (j - 1))
                turn(L, j, prev)

            def turn_qkv(L, j):
                def prev():
                    wait_read(pe, L, S_QKV + j)
                    if j >= 2:
                        pe.wait_ge(rot_read, L * 5 + (j - 1))
                    else:
                        pe.wait_ge(sgu_read, L * 4 + 4)
                turn(L, 4 + j, prev)

            def turn_rot(L, j):
                pe.wait_ge(roped, L * 5 + (j + 1))
                for t in range(TT):
                    mm = nc.tensor.transpose(aux[:, j % 2, t * P:(t + 1) * P],
                                             rot[:, j % 2, t * P:(t + 1) * P], ident[:])
                mm.then_inc(rot_turned, 1)

            def attention(L):
                def stage(which, it, i):
                    n0 = L * KT + it * 4 + i
                    if which == 0:
                        pe.wait_ge(staged, L * (KT + 1) + it * 4 + (i + 1))
                        if i == 0:
                            pe.wait_ge(rot_read, L * 5 + 5)
                            pe.wait_ge(turn_read, L * 10 + 10)
                        for n in range(4):
                            e, jp = n // 2, n % 2
                            for g in range(2):
                                mm = nc.tensor.matmul(
                                    aux[:, 0, g * HALF + n * P:g * HALF + (n + 1) * P],
                                    qs[g * HD:(g + 1) * HD, e, 2 * jp:2 * jp + 2, :],
                                    ks[g * HD:(g + 1) * HD, e, :], start=True, stop=True)
                        mm.then_inc(scored, 1)
                    elif which == 1:
                        pe.wait_ge(normed, n0 + 1)
                        pe.wait_ge(o_ready, n0 + 1)
                        for n in range(8):
                            mm = nc.tensor.transpose(aux[:, 1, n * P:(n + 1) * P], prob[:, n, :], ident[:])
                        mm.then_inc(p_turned, 1)
                    else:
                        pe.wait_ge(pt_ready, n0 + 1)
                        for e in range(2):
                            for g in range(2):
                                n = 4 * g + 2 * e
                                mm = nc.tensor.matmul(
                                    aux[g * HD:(g + 1) * HD, 1, e * 4 * CHUNK:(e + 1) * 4 * CHUNK],
                                    vst[:, (i % 2) * 2 + e, g * HD:(g + 1) * HD],
                                    probt[:, n:n + 2, :], start=True, stop=True)
                        mm.then_inc(pv_done, 1)
                return stage

            def ones_sum(src, p, done):
                for t in range(2):
                    mm = nc.tensor.matmul(aux[:, p, t * HALF:(t + 1) * HALF], ones[:],
                                          src[:, t * HALF:(t + 1) * HALF], start=True, stop=True)
                mm.then_inc(done, 1)

            def pool_mix_tile(L, j):
                pe.wait_ge(pooled_ready, L * WT + (j + 1))
                if j >= 2:
                    pe.wait_ge(ob_ready, L * WT + (j - 1))
                for t in range(2):
                    mm = nc.tensor.matmul(aux[:, j % 2, t * HALF:(t + 1) * HALF], pmix[:, j, :],
                                          pooled[:, j % 2, t * HALF:(t + 1) * HALF],
                                          start=True, stop=True)
                mm.then_inc(pool_mixed, 1)

            def sgu_mix(L, groups):
                if groups[0] == 0:
                    pe.wait_ge(vs_ready, L + 1)
                    pe.wait_ge(turn_read, L * 10 + 4)
                for g in groups:
                    if g >= 2:
                        pe.wait_ge(sgu_read, L * 4 + (g - 1))
                    for n in range(TT):
                        mm = nc.tensor.matmul(aux[:, g % 2, n * P:(n + 1) * P],
                                              vs[:, n, g * P:(g + 1) * P], sgt[:, g, :],
                                              start=True, stop=True)
                    mm.then_inc(sgu_mixed, 1)

            pe.wait_ge(consts_made, 1)
            pe.wait_ge(xsq_added, 2)
            for _ in range(WARMUP):
                nc.tensor.matmul(acc[:, 1, 0:P], ones[:], ones[:], start=True, stop=True)
            token_sums(0, 0)
            spread(0, 0)
            for k in range(KT):
                pe.wait_ge(xsq_ready, KT + k + 1)
                nc.tensor.matmul(aux[:, 1, HALF:SEQ], ones[:], EV[k % 2][:, 0:HALF],
                                 start=k == 0, stop=k == KT - 1).then_inc(x_summed, 1)
            pe.wait_ge(const_loaded, 48)
            with pe.Fori(0, LAYERS) as L:
                first_tiles(L)
                projects(L, S_GLU + 2, 6)
                for j in range(4):
                    project(L, S_VS + j, (lambda j=j: turn_v(L, j - 1)) if j else None)
                for j in range(4):
                    project(L, S_U + j, (lambda: turn_v(L, 3)) if j == 0 else None)
                for j in range(6):
                    project(L, S_QKV + j, (lambda j=j: turn_qkv(L, j - 1)) if j else
                            (lambda: sgu_mix(L, (0, 1))))
                    if j == 0:
                        sgu_mix(L, (2, 3))
                    if j >= 2:
                        turn_rot(L, j - 2)
                for j in range(4):
                    project(L, S_ZC + j, (lambda: turn_qkv(L, 5)) if j == 0 else None)
                    if j == 0:
                        turn_rot(L, 4)
                merge(L, S_MC, 1, attention(L))
                projects(L, S_ZA, 4)
                merge(L, S_MA, 2)
                for j in range(4):
                    project(L, S_P + j)
                    if j == 0:
                        pe.wait_ge(mix_loaded, L * 32 + 32)
                        pe.wait_ge(o_ready, L * KT + KT + 1)
                    if j:
                        pool_mix_tile(L, j - 1)
                project(L, S_ZB)
                pool_mix_tile(L, 3)
                for j in range(1, 4):
                    project(L, S_ZB + j)
                merge(L, S_MB, 3)
                def conv_mean():
                    pe.wait_ge(conv_summed, L + 1)
                    pe.wait_ge(ob_ready, L * 4 + 4)
                    ones_sum(sumsq, 0, d_mean)

                project(L, S_ZD, conv_mean)
                project(L, S_ZD + 1)
                pe.wait_ge(d_sumsq, L + 1)
                ones_sum(sumsq, 1, d_var)
                project(L, S_ZD + 2)
                project(L, S_ZD + 3)
                merge(L, S_MD, 4)
                projects(L, S_OUT, KT, (0,), 0)
                project(L, S_OUT + KT, lambda: token_sums(L * 2 + 2, 0), halves=(1,), mixed=1)
                project(L, S_OUT + KT + 1, lambda: spread(L * 2 + 2, 0), halves=(1,), mixed=1)
                projects(L, S_OUT + KT + 2, KT - 2, (1,), 1)

        out_v = out.rearrange("(k p) t -> p k t", p=P)

        @block.scalar
        def _(act):
            def evac(L, s, dst, func, su=0):
                act.wait_ge(unit_used, L * UNITS + UB[s + 1] + su)
                nc.scalar.activation(dst, acc[:, s % 2, :], func).then_inc(acc_read[s % 2], 1)

            def take_z(L, zi, s0, i, it=0):
                act.wait_ge(z_taken, L * 12 + it * 2 + (zi * 4 + i + 1))
                evac(L, s0 + i, EV[(s0 + i) % 2], ACT.Silu, it * 4)

            def gates(L, s0, n_taken, d0=0, d1=KT):
                if n_taken:
                    act.wait_ge(z_taken, L * 12 + n_taken + 2)
                with act.Fori(d0, d1) as d:
                    act.wait_ge(acc_read[1], L * PAIR + d + (s0 // 2 + 1))
                    act.wait_ge(unit_used, L * UNITS + d * 3 + (UB[s0] + 2))
                    nc.scalar.activation(EV[0], acc[:, 0, :], ACT.Sigmoid).then_inc(acc_read[0], 1)

            def rms_stage(stage):
                act.wait_ge(tok_summed, stage + 1)
                nc.scalar.activation(rms[:], aux[:, 0, 0:TT // 2], ACT.Sqrt, bias=epst[:],
                                     scale=1.0 / D).then_inc(rms_root, 1)

            def h_rounded(stage, t, k, it=0):
                act.wait_ge(h_scaled, stage * KT + it + (k + 1))
                settle(act)
                nc.scalar.activation(hhi[:, ds(it + k, 1), t * HALF:(t + 1) * HALF], htmp[:, k % HTMP, :],
                                     ACT.Copy).then_inc(h_hi, 1)

            act.sem_inc(acc_read[0], 1)
            act.sem_inc(acc_read[1], 1)
            act.sem_inc(z_taken, 2)
            act.sem_inc(o_ready, 1)
            act.wait_ge(consts_made, 1)
            nc.scalar.activation(nsink[:, 0:1], epst[:], ACT.Sqrt)

            def x_squared(n):
                t, k = n // KT, n % KT
                act.wait_ge(x_loaded[n // 2], 32)
                if n >= 2:
                    if n < KT + 2:
                        act.wait_ge(xsq_added, n - 1)
                    else:
                        act.wait_ge(x_summed, n - 1 - KT)
                nc.scalar.activation(EV[n % 2][:, 0:HALF], xm[:, k, t * HALF:(t + 1) * HALF],
                                     ACT.Square).then_inc(xsq_ready, 1)

            for n in range(KT):
                x_squared(n)
            rms_stage(0)
            for squares, tiles_h in (((0, 1), (0, 1)), ((2, 3), (2, 3)), ((4, 5, 6, 7), (4, 5))):
                for k in squares:
                    x_squared(KT + k)
                for k in tiles_h:
                    h_rounded(0, 0, k)
            act.wait_ge(x_summed, KT)
            nc.scalar.activation(sumsq[:, HALF:SEQ], aux[:, 1, HALF:SEQ], ACT.Copy,
                                 scale=1.0 / P).then_inc(xsq_added, KT)
            for k in (6, 7):
                h_rounded(0, 0, k)
            act.wait_ge(const_loaded, 48)
            act.dma_start(out, x).then_inc(x_copied, 16)

            with act.Fori(0, LAYERS) as L:
                nc.scalar.activation(par[:], allp[:].rearrange("p l n -> p (l n)")[:, ds(L * C_N, C_N)],
                                     ACT.Copy).then_inc(par_ready, 1)
                rms_stage(L * 2 + 1)
                with act.Fori(0, KT // HTMP) as it:
                    for i in range(HTMP):
                        h_rounded(L * 2 + 1, 1, i, it * HTMP)
                act.dma_start(rowb[:], rows[ds(L, 1), :].partition_broadcast(P)).then_inc(rows_loaded, 16)
                act.dma_start(sgt[:], sgu_wt[ds(L, 1)]).then_inc(rows_loaded, 16)
                act.wait_ge(h_ready, L * 2 * KT + 2 * KT)
                act.dma_start(cosb[:], rope[0]).then_inc(rope_loaded, 16)
                act.dma_start(sinb[:], rope[1]).then_inc(rope_loaded, 16)
                with act.Fori(0, WT) as j:
                    act.wait_ge(acc_read[1], L * PAIR + j + 1)
                    act.wait_ge(unit_used, L * UNITS + j * 4 + 2)
                    nc.scalar.activation(EV[0], acc[:, 0, :], ACT.Sigmoid).then_inc(acc_read[0], 1)
                act.wait_ge(acc_read[1], L * PAIR + (S_VS // 2 + 1))
                for j in range(4):
                    if j >= 2:
                        act.wait_ge(turned, L * 10 + (j - 1))
                    evac(L, S_VS + j, EV[j % 2], ACT.Copy)
                for j in range(4):
                    evac(L, S_U + j, oc[:, j, :], ACT.Copy)
                    if j == 2:
                        act.wait_ge(sgu_var, L + 1)
                        nc.scalar.activation(st[:, 0, :], mv[:, :, 1], ACT.Sqrt,
                                             bias=epst[:]).then_inc(sgu_root, 1)

                def take_turned(j):
                    act.wait_ge(turned, L * 10 + (j + 5))
                    if j == 5:
                        nc.scalar.activation(vt[:], aux[:, 1, :], ACT.Copy).then_inc(turn_read, 1)
                        return
                    if j:
                        act.wait_ge(roped, L * 5 + j)
                    nc.scalar.activation(tok[:], aux[:, j % 2, :], ACT.Copy)
                    nc.scalar.activation(sqt[:], aux[:, j % 2, :], ACT.Square).then_inc(turn_read, 1)
                    act.wait_ge(qk_meansq, L * 5 + (j + 1))
                    nc.scalar.activation(stq[:, 1, :], stq[:, 0, :], ACT.Sqrt, bias=epst[:],
                                         scale=1.0 / HD).then_inc(qk_root, 1)

                def take_rotated(j):
                    act.wait_ge(rot_turned, L * 5 + (j + 1))
                    dst = kt[:] if j == NQT else qo[:, j, :]
                    nc.scalar.activation(dst, aux[:, j % 2, :], ACT.Copy).then_inc(rot_read, 1)

                for j in range(7):
                    if j:
                        take_turned(j - 1)
                    if j < 6:
                        act.wait_ge(turned, L * 10 + (4 if j < 2 else j + 3))
                        evac(L, S_QKV + j, EV[j % 2], ACT.Copy)
                    else:
                        take_z(L, 0, S_ZC, 0)
                    if j >= 2:
                        take_rotated(j - 2)
                def stage_qk(m, prev):
                    for e in range(2):
                        nc.scalar.activation(qs[:, e, :, :],
                                             qo[:, :, ds(m * P + e * CHUNK, CHUNK)], ACT.Copy)
                    nc.scalar.activation(ks[:, 0, 0:CHUNK], kt[:, ds(m * P, CHUNK)], ACT.Copy)
                    nc.scalar.activation(ks[:, 0, CHUNK:P], kt[:, ds(prev * CHUNK, CHUNK)], ACT.Copy)
                    nc.scalar.activation(ks[:, 1, :], kt[:, ds(m * P, P)], ACT.Copy).then_inc(staged, 1)

                for j in range(1, 4):
                    if j == 3:
                        act.wait_ge(rot_read, L * 5 + 5)
                        stage_qk(0, NCHUNK - 1)
                    take_z(L, 0, S_ZC, j)

                act.wait_ge(z_taken, L * 12 + (4 + 2))
                act.wait_ge(turn_read, L * 10 + 10)
                with act.Fori(0, 2) as it:
                    for i in range(4):
                        s = S_MC + 2 * i
                        pt = it * (-4) + 7 if i == 0 else it * 4 + (i - 1)
                        v0 = (i % 2) * 2
                        nc.scalar.activation(vst[0:CHUNK, v0, :], vt[0:CHUNK, ds(it * 4 + i, 1), :], ACT.Copy)
                        nc.scalar.activation(vst[CHUNK:P, v0, :], vt[CHUNK:P, ds(pt, 1), :], ACT.Copy)
                        nc.scalar.activation(vst[:, v0 + 1, :], vt[:, ds(it * 4 + i, 1), :], ACT.Copy)
                        act.wait_ge(rowmax, L * KT + it * 4 + (i + 1))
                        for n in range(8):
                            nc.scalar.activation(
                                prob[:, n, :], aux[:, 0, n * P:(n + 1) * P], ACT.Exp,
                                bias=st[:, NMAX, n:n + 1], scale=SCALE, accum_out=st[:, PSUM_, n:n + 1])
                        nc.scalar.activation(st[:, ESINK, :], st[:, SDIFF, :], ACT.Exp).then_inc(probs_ready, 1)
                        if i < 3:
                            stage_qk(it * 4 + (i + 1), it * 8 + (2 * i + 1))
                        else:
                            stage_qk(it * (-4) + 4, 7)
                        act.wait_ge(acc_read[1], L * PAIR + it * 4 + (s // 2 + 1))
                        act.wait_ge(unit_used, L * UNITS + it * 12 + (UB[s] + 2))
                        nc.scalar.activation(EV[0], acc[:, 0, :], ACT.Sigmoid).then_inc(acc_read[0], 1)
                wait_read(act, L, S_ZA - 1)
                with act.Fori(0, 2) as it:
                    for i in range(2):
                        take_z(L, 1, S_ZA, i, it)
                gates(L, S_MA, 8)
                act.wait_ge(unit_used, used(L, S_P))
                act.dma_start(pmix[:], pool_mix[ds(L, 1)]).then_inc(mix_loaded, 16)
                act.dma_start(edge[:], edge_in).then_inc(mix_loaded, 16)
                wait_read(act, L, S_P - 1)

                def take_mixed(j):
                    act.wait_ge(pool_mixed, L * WT + (j + 1))
                    nc.scalar.activation(oc[:, j, :], aux[:, j % 2, :], ACT.Copy,
                                         scale=par[:, C_PS + j:C_PS + j + 1]).then_inc(ob_ready, 1)

                for j in range(4):
                    if j >= 2:
                        act.wait_ge(pooled_ready, L * WT + (j - 1))
                    evac(L, S_P + j, EV[j % 2], ACT.Copy)
                    if j:
                        take_mixed(j - 1)
                act.wait_ge(pooled_ready, L * WT + WT)
                take_z(L, 2, S_ZB, 0)
                take_mixed(3)
                for j in range(1, 4):
                    take_z(L, 2, S_ZB, j)
                gates(L, S_MB, 12)
                act.wait_ge(z_taken, L * 12 + (12 + 2))
                wait_read(act, L, S_ZD - 1)
                evac(L, S_ZD, oc[:, 0, :], ACT.Silu)
                for j in range(WT):
                    act.wait_ge(d_centred, L * WT + (j + 1))
                    nc.scalar.activation(csq[:, j, :], conv[:, j, PADC:PADC + SEQ],
                                         ACT.Square).then_inc(d_squared, 1)
                evac(L, S_ZD + 1, oc[:, 1, :], ACT.Silu)
                act.wait_ge(d_var, L + 1)
                nc.scalar.activation(conv[:, WT, PADC:PADC + SEQ], aux[:, 1, :], ACT.Sqrt,
                                     bias=epst[:], scale=1.0 / W).then_inc(d_root, 1)
                evac(L, S_ZD + 2, oc[:, 2, :], ACT.Silu)
                for j in range(WT):
                    act.wait_ge(d_normed, L * WT + (j + 1))
                    nc.scalar.activation(csq[:, j, :], conv[:, j, PADC:PADC + SEQ], ACT.Silu,
                                         bias=par[:, C_CLB + j:C_CLB + j + 1],
                                         scale=par[:, C_CLG + j:C_CLG + j + 1]).then_inc(d_act, 1)
                evac(L, S_ZD + 3, oc[:, 3, :], ACT.Silu)
                act.wait_ge(gated, L * 16 + 16)
                act.wait_ge(x_copied, 16)
                act.dma_start(xin[:], out_v).then_inc(xin_loaded, 16)
                gates(L, S_MD, 0, 0, KT - 1)

                def mix_rounded(t, d0, d1):
                    with act.Fori(d0, d1) as d:
                        act.wait_ge(merged, L * (KT + 1) + d + 1 + t)
                        settle(act)
                        nc.scalar.activation(hhi[:, ds(d, 1), t * HALF:(t + 1) * HALF],
                                             xm[:, ds(d, 1), t * HALF:(t + 1) * HALF],
                                             ACT.Copy).then_inc(mix_hi, 1)

                act.wait_ge(unit_used, used(L, S_MD + 2 * KT - 1))
                settle(act)
                mix_rounded(0, 0, KT - 2)
                gates(L, S_MD, 0, KT - 1, KT)
                mix_rounded(0, KT - 2, KT)
                mix_rounded(1, 0, KT)

                def new_x(t, i, it=0):
                    s = S_OUT + t * KT + i
                    here = xm[:, ds(it * 2 + i, 1), t * HALF:(t + 1) * HALF]
                    act.wait_ge(acc_read[i % 2], L * PAIR + it + (s // 2 + 2))
                    act.dma_start(out_v[:, ds(it * 2 + i, 1), t * HALF:(t + 1) * HALF],
                                  here).then_inc(x_stored, 16)
                    act.wait_ge(xsq_added, L * 2 * KT + it * 2 + (2 * KT + t * KT + i - 1))
                    settle(act)
                    nc.scalar.activation(EV[i % 2][:, 0:HALF], here, ACT.Square).then_inc(xsq_ready, 1)

                with act.Fori(0, KT // 2) as it:
                    for i in range(2):
                        new_x(0, i, it)
                rms_stage(L * 2 + 2)
                for d in range(KT):
                    new_x(1, d)
                    for k in H_TILES[d]:
                        h_rounded(L * 2 + 2, 0, k)
                act.wait_ge(x_stored, L * (32 * KT) + 32 * KT)

        @block.vector
        def _(dve):
            def mul(out, a, b):
                return nc.vector.tensor_tensor(out, a, b, ALU.mult)

            def add(out, a, b):
                return nc.vector.tensor_tensor(out, a, b, ALU.add)

            def gate_tile(L, src, z, j_src, j_dst):
                mul(src[:, ds(j_src, 1), :], z, src[:, ds(j_src, 1), :]).then_inc(z_taken, 1)
                split_tile(src[:, ds(j_src, 1), :], j_dst)

            def split_tile(tile, j):
                dve.drain()
                nc.vector.tensor_copy(bhi[:, ds(j, 1), :], tile)
                dve.drain()
                nc.vector.tensor_tensor(blo[:, ds(j, 1), :], tile, bhi[:, ds(j, 1), :].bitcast(F32),
                                        ALU.subtract).then_inc(gated, 1)

            def rms_invert(stage):
                rms_diagonals(stage)
                rms_everywhere(stage)

            def rms_diagonals(stage):
                dve.wait_ge(rms_root, stage + 1)
                nc.vector.reciprocal(rms[:], rms[:])
                dve.drain()
                mul(diag[:], ident[:].unsqueeze(1).to_broadcast([P, TT // 2, P]),
                    rms[:].unsqueeze(2).to_broadcast([P, TT // 2, P])).then_inc(rms_diag, 1)

            def rms_everywhere(stage):
                dve.wait_ge(rms_spread, stage + 1)
                settle(dve)

            def h_scale(gains, t, k, it=0):
                nc.vector.scalar_tensor_tensor(
                    out=htmp[:, k % HTMP, :], in0=xm[:, ds(it + k, 1), t * HALF:(t + 1) * HALF],
                    scalar=allf[:, ds(gains + it + (C_G + k), 1)], in1=aux[:, 1, t * HALF:(t + 1) * HALF],
                    op0=ALU.mult, op1=ALU.mult).then_inc(h_scaled, 1)

            def h_rest(stage, t, k, it=0):
                dve.wait_ge(h_hi, stage * KT + it + (k + 1))
                here = (slice(None), ds(it + k, 1), slice(t * HALF, (t + 1) * HALF))
                nc.vector.tensor_tensor(hlo[here], htmp[:, k % HTMP, :], hhi[here].bitcast(F32),
                                        ALU.subtract).then_inc(h_ready, 1)

            def h_group(gains, stage, t, it=0):
                dve.drain()
                for k in range(HTMP + 2):
                    if k < HTMP:
                        h_scale(gains, t, k, it)
                    if k >= 2:
                        h_rest(stage, t, k - 2, it)

            def square_added(n, t, i):
                dve.wait_ge(xsq_ready, n)
                half = sumsq[:, t * HALF:(t + 1) * HALF]
                add(half, half, EV[i][:, 0:HALF]).then_inc(xsq_added, 1)
                dve.drain()

            allf = allp[:].rearrange("p l n -> p (l n)")

            def gate_loop(L, src, s0):
                with dve.Fori(0, 2) as it:
                    for i in range(2):
                        s = s0 + i
                        dve.wait_ge(acc_read[i], L * PAIR + it + (s // 2 + 2))
                        gate_tile(L, src, EV[i], it * 2 + i, it * 2 + i)

            def merge_tile(L, s0, d, tmp, done=None):
                dve.drain()
                dve.wait_ge(acc_read[0], L * PAIR + d + (s0 // 2 + 2))
                dve.wait_ge(unit_used, L * UNITS + d * 3 + (UB[s0] + 3))
                if tmp is None:
                    mul(xm[:, ds(d, 1), :], EV[0], acc[:, 1, :]).then_inc(acc_read[1], 1)
                    return
                mul(tmp, EV[0], acc[:, 1, :]).then_inc(acc_read[1], 1)
                dve.drain()
                last = add(xm[:, ds(d, 1), :], xm[:, ds(d, 1), :], tmp)
                if done is not None:
                    last.then_inc(done, 1)

            convf = conv[:].rearrange("p s t -> p (s t)")
            SW = PADC + SEQ

            def conv_merge(L, s0, j0):
                with dve.Fori(0, 2) as it:
                    for i in range(4):
                        o = convf[:, ds(it * SW + (j0 * SW + PADC), SEQ)]
                        for k in range(8 * i, min(8 * i + 8, TAPS)):
                            h = convf[:, ds(it * SW + ((j0 + 1) * SW + PADC - (TAPS - 1) + k), SEQ)]
                            w = par[:, ds(it * TAPS + (C_CW + j0 * TAPS + k), 1)]
                            if k == 0:
                                nc.vector.tensor_scalar(o, h, w, par[:, ds(it + (C_CB + j0), 1)],
                                                        ALU.mult, ALU.add)
                            else:
                                nc.vector.scalar_tensor_tensor(out=o, in0=h, scalar=w, in1=o,
                                                               op0=ALU.mult, op1=ALU.add)
                            dve.drain()
                        merge_tile(L, s0, it * 4 + i, oc[:, 0, :])

            for t in (ev[:, :, 0:POOL_PAD], conv[:, :, 0:PADC], sumsq[:]):
                nc.vector.memset(t, 0.0)
            nc.vector.memset(ones[:], 1.0)
            nc.vector.memset(epst[:], EPS)
            dve.drain()
            nc.vector.memset(st[:], 0.0).then_inc(consts_made, 1)
            for n in range(KT):
                square_added(n + 1, 0, n % 2)
            dve.wait_ge(const_loaded, 48)
            rms_invert(0)
            for k in range(0, KT, HTMP):
                h_group(0, 0, 0, k)

            with dve.Fori(0, LAYERS) as L:
                rms_invert(L * 2 + 1)
                with dve.Fori(0, KT // HTMP) as it:
                    h_group(L * C_N, L * 2 + 1, 1, it * HTMP)
                dve.wait_ge(par_ready, L + 1)
                nc.vector.tensor_scalar(nsink[:], par[:, C_SINK:C_SINK + 8], -1.0, None, ALU.mult)
                with dve.Fori(0, WT) as j:
                    dve.wait_ge(acc_read[0], L * PAIR + j + 2)
                    dve.wait_ge(unit_used, L * UNITS + j * 4 + 4)
                    mul(convf[:, ds(j * SW + (SW + PADC), SEQ)], acc[:, 1, :],
                        EV[0]).then_inc(acc_read[1], 1)
                for j in range(4):
                    dve.wait_ge(turned, L * 10 + (j + 1))
                    nc.vector.tensor_copy(vs[:, :, j * P:(j + 1) * P],
                                          aux[:, j % 2, :].rearrange("p (t c) -> p t c", c=P)
                                          ).then_inc(turn_read, 1)
                dve.drain()
                for t in range(TT):
                    nc.vector.bn_stats(stv[:, t, :], vs[:, t, :])
                dve.drain()
                for t in range(TT):
                    last = nc.vector.bn_aggr(mv[:, t, :], stv[:, t, :])
                last.then_inc(sgu_var, 1)
                dve.wait_ge(rows_loaded, L * 32 + 32)
                nc.vector.memset(sgt[CHUNK:P, :, 0:CHUNK], 0.0)
                dve.wait_ge(rope_loaded, L * 32 + 32)
                for q in range(2):
                    for n, (t, half) in enumerate(((cosb, 0), (sinb, 1), (cosb, 1), (sinb, 0))):
                        g0 = R_QK + q * HD + half * (HD // 2)
                        g = rowb[:, g0:g0 + HD // 2].unsqueeze(1).to_broadcast([P, TT, HD // 2])
                        mul(ropeb[:, q, n, :, :], t[:], g)
                dve.wait_ge(sgu_root, L + 1)
                nc.vector.reciprocal(st[:, 1, :], st[:, 0, :])
                dve.drain()
                for t in range(TT):
                    nc.vector.tensor_scalar(vs[:, t, :], vs[:, t, :], mv[:, t, 0:1], st[:, 1, t:t + 1],
                                            ALU.subtract, ALU.mult)
                dve.drain()
                mul(vs[:], vs[:], rowb[:, R_G:R_G + W].unsqueeze(1).to_broadcast([P, TT, W]))
                dve.drain()
                add(vs[:], vs[:], rowb[:, R_B:R_B + W].unsqueeze(1).to_broadcast([P, TT, W])
                    ).then_inc(vs_ready, 1)
                wait_read(dve, L, S_U + 2)
                wait_read(dve, L, S_U + 3)
                for g in range(4):
                    dve.wait_ge(sgu_mixed, L * 4 + (g + 1))
                    bs = rowb[:, R_BS + g * P:R_BS + (g + 1) * P].unsqueeze(1).to_broadcast([P, TT, P])
                    add(stmp[:].rearrange("p (n i) -> p n i", i=P),
                        aux[:, g % 2, :].rearrange("p (n i) -> p n i", i=P), bs).then_inc(sgu_read, 1)
                    dve.drain()
                    mul(oc[:, g, :], stmp[:], oc[:, g, :])
                    dve.drain()
                v4 = tok[:].rearrange("p (t h a d) -> p t h a d", t=TT, h=2, a=2)
                f1 = rt1[:].rearrange("p (t h d) -> p t h d", t=TT, h=2)
                f2 = rt2[:].rearrange("p (t h d) -> p t h d", t=TT, h=2)
                for j in range(5):
                    dve.drain()
                    tab = [ropeb[:, j // NQT, n, :, :].unsqueeze(2).to_broadcast([P, TT, 2, HD // 2])
                           for n in range(4)]
                    r4 = rot[:, j % 2, :].rearrange("p (t h a d) -> p t h a d", t=TT, h=2, a=2)
                    dve.wait_ge(turn_read, L * 10 + (j + 5))
                    nc.vector.tensor_reduce(stq[:, 0, :], sqt[:].rearrange("p (n d) -> p n d", d=HD),
                                            AX.X, ALU.add).then_inc(qk_meansq, 1)
                    dve.wait_ge(qk_root, L * 5 + (j + 1))
                    nc.vector.reciprocal(stq[:, 1, :], stq[:, 1, :])
                    dve.drain()
                    tn = tok[:].rearrange("p (n d) -> p n d", d=HD)
                    mul(tn, tn, stq[:, 1, :].unsqueeze(2).to_broadcast([P, NPAIRS, HD]))
                    dve.drain()
                    if j >= 2:
                        dve.wait_ge(rot_turned, L * 5 + (j - 1))
                    mul(f1, v4[:, :, :, 0, :], tab[0])
                    mul(f2, v4[:, :, :, 1, :], tab[1])
                    dve.drain()
                    nc.vector.tensor_tensor(r4[:, :, :, 0, :], f1, f2, ALU.subtract)
                    dve.drain()
                    mul(f1, v4[:, :, :, 1, :], tab[2])
                    mul(f2, v4[:, :, :, 0, :], tab[3])
                    dve.drain()
                    add(r4[:, :, :, 1, :], f1, f2).then_inc(roped, 1)
                gate_loop(L, oc, S_ZC)

                with dve.Fori(0, 2) as it:
                    for i in range(4):
                        n0 = L * KT + it * 4 + i
                        dve.wait_ge(scored, n0 + 1)
                        sc = aux[:, 0, :].rearrange("p (n k) -> p n k", k=P)
                        if i == 0:
                            m = mask[:, ds(it, 1), :].to_broadcast([P, 2, CHUNK])
                            for g in range(2):
                                s0 = sc[:, 4 * g:4 * g + 2, CHUNK:P]
                                add(s0, s0, m)
                            dve.drain()
                        nc.vector.tensor_reduce(st[:, MAXS, :], sc, AX.X, ALU.max)
                        dve.drain()
                        nc.vector.scalar_tensor_tensor(
                            out=st[:, NMAX, :], in0=st[:, MAXS, :], scalar=-SCALE,
                            in1=nsink[:], op0=ALU.mult, op1=ALU.min)
                        dve.drain()
                        nc.vector.tensor_tensor(st[:, SDIFF, :], st[:, NMAX, :], nsink[:],
                                                ALU.subtract).then_inc(rowmax, 1)
                        dve.wait_ge(probs_ready, n0 + 1)
                        add(st[:, DEN, :], st[:, PSUM_, :], st[:, ESINK, :])
                        dve.drain()
                        nc.vector.reciprocal(st[:, RDEN, :], st[:, DEN, :])
                        dve.drain()
                        mul(prob[:], prob[:],
                            st[:, RDEN, :].unsqueeze(2).to_broadcast([P, 8, P])).then_inc(normed, 1)
                        dve.wait_ge(p_turned, n0 + 1)
                        nc.vector.tensor_copy(probt[:].rearrange("p n q -> p (n q)"),
                                              aux[:, 1, :]).then_inc(pt_ready, 1)
                        dve.wait_ge(pv_done, n0 + 1)
                        nc.vector.tensor_copy(
                            qo[:, :, ds((it * 4 + i) * P, P)].rearrange("p n (e q) -> p e n q", e=2),
                            aux[:, 1, 0:8 * CHUNK].rearrange("p (e n q) -> p e n q", e=2, n=4)
                        ).then_inc(o_ready, 1)
                        merge_tile(L, S_MC, it * 4 + i, None)
                dve.drain()
                gate_loop(L, qo, S_ZA)
                conv_merge(L, S_MA, 0)
                cv = [conv[:, j, PADC:SW] for j in range(WT + 1)]
                dve.drain()
                add(sumsq[:], cv[0], cv[1])

                dve.wait_ge(mix_loaded, L * 32 + 32)
                nc.vector.memset(pool1[:, 0:POOL_PAD], 0.0)
                nc.vector.memset(pool2[:, 0:POOL_PAD], 0.0)
                dve.drain()
                for j, w in enumerate(POOL_W):
                    dve.drain()
                    wait_read(dve, L, S_P + j)
                    src = ev[:, j % 2, :]
                    shift = 1
                    bufs = [pool1, pool2]
                    while shift < w:
                        if shift > 1:
                            dve.drain()
                        dst = bufs.pop(0)
                        bufs.append(dst)
                        add(dst[:, POOL_PAD:], src[:, POOL_PAD:],
                            src[:, POOL_PAD - shift:POOL_PAD - shift + SEQ])
                        src, shift = dst, 2 * shift
                    dve.drain()
                    if j >= 2:
                        dve.wait_ge(pool_mixed, L * WT + (j - 1))
                    nc.vector.scalar_tensor_tensor(out=pooled[:, j % 2, :], in0=src[:, POOL_PAD:],
                                                   scalar=1.0 / w, in1=EV[j % 2], op0=ALU.mult,
                                                   op1=ALU.subtract)
                    dve.drain()
                    mul(pooled[:, j % 2, 0:POOL_PAD], src[:, POOL_PAD:2 * POOL_PAD], edge[:, j, :])
                    dve.drain()
                    nc.vector.tensor_tensor(pooled[:, j % 2, 0:POOL_PAD], pooled[:, j % 2, 0:POOL_PAD],
                                            EV[j % 2][:, 0:POOL_PAD], ALU.subtract).then_inc(pooled_ready, 1)
                dve.wait_ge(ob_ready, L * WT + WT)
                settle(dve)
                gate_loop(L, oc, S_ZB)
                conv_merge(L, S_MB, 2)

                dve.drain()
                add(sumsq[:], sumsq[:], cv[2])
                dve.drain()
                add(sumsq[:], sumsq[:], cv[3]).then_inc(conv_summed, 1)
                dve.wait_ge(d_mean, L + 1)
                for j in range(WT):
                    nc.vector.scalar_tensor_tensor(out=cv[j], in0=aux[:, 0, :], scalar=-1.0 / W,
                                                   in1=cv[j], op0=ALU.mult,
                                                   op1=ALU.add).then_inc(d_centred, 1)
                dve.wait_ge(d_squared, L * WT + 2)
                add(sumsq[:], csq[:, 0, :], csq[:, 1, :])
                dve.drain()
                dve.wait_ge(d_squared, L * WT + 3)
                add(sumsq[:], sumsq[:], csq[:, 2, :])
                dve.drain()
                dve.wait_ge(d_squared, L * WT + 4)
                add(sumsq[:], sumsq[:], csq[:, 3, :]).then_inc(d_sumsq, 1)
                dve.wait_ge(d_root, L + 1)
                nc.vector.reciprocal(cv[WT], cv[WT])
                dve.drain()
                for j in range(WT):
                    mul(cv[j], cv[j], cv[WT]).then_inc(d_normed, 1)
                nc.vector.memset(sumsq[:], 0.0)
                dve.wait_ge(unit_used, used(L, S_ZD))
                for j in range(WT):
                    wait_read(dve, L, S_ZD + j)
                    dve.wait_ge(d_act, L * WT + (j + 1))
                    mul(csq[:, j, :], csq[:, j, :], oc[:, j, :])
                    split_tile(csq[:, j:j + 1, :], j)
                with dve.Fori(0, KT - 1) as d:
                    merge_tile(L, S_MD, d, cv[WT], merged)

                def mix_rest(t, d):
                    dve.wait_ge(mix_hi, L * 2 * KT + d + (t * KT + 1))
                    here = (slice(None), ds(d, 1), slice(t * HALF, (t + 1) * HALF))
                    nc.vector.tensor_tensor(hlo[here], xm[here], hhi[here].bitcast(F32),
                                            ALU.subtract).then_inc(mix_ready, 1)

                dve.drain()
                with dve.Fori(0, KT - 2) as d:
                    mix_rest(0, d)
                dve.wait_ge(acc_read[0], L * PAIR + (KT - 1 + S_MD // 2 + 2))
                dve.wait_ge(unit_used, used(L, S_MD + 2 * KT))
                for t in range(2):
                    here = (slice(None), slice(t * HALF, (t + 1) * HALF))
                    last = mul(cv[WT][here], EV[0][here], acc[:, 1, t * HALF:(t + 1) * HALF])
                    if t == 1:
                        last.then_inc(acc_read[1], 1)
                    dve.drain()
                    add(xm[:, KT - 1, t * HALF:(t + 1) * HALF], xm[:, KT - 1, t * HALF:(t + 1) * HALF],
                        cv[WT][here]).then_inc(merged, 1)
                    if t == 0:
                        mix_rest(0, KT - 2)
                        mix_rest(0, KT - 1)
                with dve.Fori(0, KT) as d:
                    mix_rest(1, d)

                def new_x(t, i, it=0, between=None):
                    s = S_OUT + t * KT + i
                    dve.wait_ge(unit_used, L * UNITS + it * 4 + UB[s + 1])
                    here = (slice(None), ds(it * 2 + i, 1), slice(t * HALF, (t + 1) * HALF))
                    add(xm[here], acc[:, i % 2, t * HALF:(t + 1) * HALF],
                        xin[here]).then_inc(acc_read[i % 2], 1)
                    if between:
                        between()
                    square_added(L * 2 * KT + it * 2 + (2 * KT + t * KT + i + 1), t, i % 2)

                dve.wait_ge(xin_loaded, L * 16 + 16)
                settle(dve)
                with dve.Fori(0, KT // 2) as it:
                    for i in range(2):
                        new_x(0, i, it)
                rms_diagonals(L * 2 + 2)
                for d in range(KT):
                    def scale_next():
                        if d == 1:
                            rms_everywhere(L * 2 + 2)
                        for k in H_TILES[d]:
                            h_scale(L * C_N + C_N, 0, k)

                    new_x(1, d, between=scale_next)
                    for k in H_TILES[d]:
                        h_rest(L * 2 + 2, 0, k)
                    dve.drain()


def column_tiles():
    names = ["q", "k", "v", "za", "p", "zb", "u", "vs", "zc", "ga", "gb", "zd"]
    sizes = [W, P, P, W, W, W, W, W, W, W, W, W]
    at = dict(zip(names, [sum(sizes[:i]) for i in range(len(sizes))]))
    return at, sum(sizes)


def kernel(**inputs):
    import numpy as np
    import concourse.bacc as bacc
    from concourse.bass_utils import run_bass_kernel_spmd

    a = {k: np.asarray(v) for k, v in inputs.items()}
    at, merge0 = column_tiles()

    def pair_cols(base, j):
        return np.concatenate([np.arange(base + j * HD, base + (j + 1) * HD),
                               np.arange(base + (j + 4) * HD, base + (j + 5) * HD)])

    def plain(base, j):
        return np.arange(base + j * P, base + (j + 1) * P)

    def units(w):
        k = w.shape[0] // W
        return w.reshape(k, UK, P, P).transpose(0, 2, 1, 3).reshape(k, P, UW)

    perm = np.concatenate([pair_cols(0, j) for j in range(4)])
    stream = []
    for l in range(LAYERS):
        w_in, w_br, w_out = a["w_in"][l], a["w_branch"][l], a["w_out"][l]

        def proj(cols):
            stream.append(units(w_in[:, cols]))

        def merge(n):
            wb = w_br[n][perm] if n == 0 else w_br[n]
            for d in range(KT):
                proj(plain(merge0 + n * D, d))
                stream.append(units(wb[:, d * P:(d + 1) * P]))

        for j in range(4):
            proj(plain(at["gb"], j))
            proj(plain(at["ga"], j))
        for n in ("vs", "u"):
            for j in range(4):
                proj(plain(at[n], j))
        for j in range(4):
            proj(pair_cols(at["q"], j))
        proj(plain(at["k"], 0))
        proj(plain(at["v"], 0))
        for j in range(4):
            proj(plain(at["zc"], j))
        merge(2)
        for j in range(4):
            proj(pair_cols(at["za"], j))
        merge(0)
        for n in ("p", "zb"):
            for j in range(4):
                proj(plain(at[n], j))
        merge(1)
        for j in range(4):
            proj(plain(at["zd"], j))
        merge(3)
        for d in list(range(KT)) * 2:
            stream.append(units(w_out[:, d * P:(d + 1) * P]))
    wstream = np.ascontiguousarray(np.concatenate(stream))
    assert wstream.shape[0] == LAYERS * UNITS

    def tiles(v):
        return np.moveaxis(v.reshape(*v.shape[:-1], -1, P), -1, 0)

    cols = []
    for l in range(LAYERS):
        cw = a["conv_w"][l]
        cwt = cw.reshape(TAPS, WT, P).transpose(2, 1, 0).reshape(P, WT * TAPS)
        sk = a["attn_sinks"][l].reshape(2, 2, 2)
        sink = np.broadcast_to(sk.transpose(2, 0, 1)[:, :, None, :], (2, 2, 2, 2)).reshape(2, 8)
        sink = np.repeat(sink, CHUNK, axis=0)
        cols.append(np.concatenate([tiles(a["norm_g"][l]), cwt, tiles(a["conv_b"][l]),
                                    tiles(a["conv_ln_g"][l]), tiles(a["conv_ln_b"][l]),
                                    tiles(a["pool_scale"][l]), sink], axis=1))
    cols = np.ascontiguousarray(np.stack(cols + [np.zeros_like(cols[0])], 1))
    rows = np.ascontiguousarray(np.concatenate(
        [a["sgu_ln_g"], a["sgu_ln_b"], a["sgu_b"].reshape(LAYERS, W), a["q_norm_g"], a["k_norm_g"]], 1))
    sgu_wt = np.ascontiguousarray(a["sgu_w"].transpose(0, 3, 1, 2))
    pool_mix = np.ascontiguousarray(a["pool_mix"].transpose(0, 2, 1, 3))
    pos = np.arange(SEQ, dtype=np.float32)
    inv = (1.0 / (np.float32(10000.0) ** (np.arange(0, HD, 2, dtype=np.float32) / np.float32(HD)))
           ).astype(np.float32)
    ang = (pos[:, None] * inv[None, :]).astype(np.float32).astype(np.float64)
    rope = np.ascontiguousarray(np.stack([
        t.astype(np.float32).reshape(TT, P, HD // 2).transpose(1, 0, 2)
        for t in (np.cos(ang), np.sin(ang))]))
    ident = np.eye(P, dtype=np.float32)
    mask = np.zeros((P, 2, CHUNK), np.float32)
    mask[:, 0] = NEG
    edge = np.stack([1.0 / np.minimum(np.arange(1, POOL_PAD + 1), w) for w in POOL_W]).astype(np.float32)
    edge = np.ascontiguousarray(np.broadcast_to(edge, (P, WT, POOL_PAD)))

    arrays = {"x": np.ascontiguousarray(a["x"][0].T), "wstream": wstream, "cols": cols, "rows": rows,
              "sgu_wt": sgu_wt, "pool_mix": pool_mix, "rope": rope, "ident": ident, "mask_in": mask,
              "edge_in": edge}
    nc = bacc.Bacc("TRN2", target_bir_lowering=False, num_devices=1, dynamic_dma_scratch_size=1024)
    args = [nc.dram_tensor(k, v.shape, mybir.dt.from_np(v.dtype), kind="ExternalInput").ap()
            for k, v in arrays.items()]
    res = nc.dram_tensor("out", (D, SEQ), F32, kind="ExternalOutput").ap()
    hybrid_block(nc, *args, res)
    r = run_bass_kernel_spmd(nc, [arrays], core_ids=[0])
    return np.ascontiguousarray(r.results[0]["out"].T)[None]
```
